# Optimizing a Trainium2 kernel written in Bass

```python
import math
import jax, jax.numpy as jnp
from jax import lax
import numpy as np

D_MODEL = 1024
BATCH = 1
SEQ = 256
DEPTH = 2
DEC_BATCH = 8
DEC_SEQ = 1
PAST_LEN = 2048
PAGE_SIZE = 128

POOL_WIDTH = D_MODEL // 2
LRU_WIDTH = D_MODEL - POOL_WIDTH
MIX_WIDTH = POOL_WIDTH + LRU_WIDTH
IN_WIDTH = POOL_WIDTH + 2 * LRU_WIDTH
POOL_WINDOWS = (2, 4, 8, 16)
N_POOL_GROUPS = len(POOL_WINDOWS)
POOL_GROUP_DIM = POOL_WIDTH // N_POOL_GROUPS
POOL_BUF = max(POOL_WINDOWS) - 1
N_LRU_HEADS = 8
LRU_HEAD_DIM = LRU_WIDTH // N_LRU_HEADS
CONV_WIDTH = 4
LRU_C = 8.0
D_FF = 128 * int(round(8 * D_MODEL / 3 / 128))
N_MOD = 9
ALPHA = (2 * DEPTH) ** 0.25
BETA = (8 * DEPTH) ** -0.25
LN_EPS = 1e-5

kernel_name = "hybrid_pool_rglru_macaron_deepnorm_step"

def layer_norm(x, g, b):
    xf = x.astype(jnp.float32)
    mu = jnp.mean(xf, -1, keepdims=True)
    var = jnp.mean(jnp.square(xf - mu), -1, keepdims=True)
    y = (xf - mu) * lax.rsqrt(var + LN_EPS)
    return (y * g.astype(jnp.float32) + b.astype(jnp.float32)).astype(x.dtype)

def modulate(x, shift, scale):
    return x * (1.0 + scale[:, None, :]) + shift[:, None, :]

def swiglu(h, w_gu, w_down):
    gu = jnp.einsum('bld,df->blf', h, w_gu)
    g, u = jnp.split(gu, 2, axis=-1)
    return jnp.einsum('blf,fd->bld', jax.nn.silu(g) * u, w_down)

def pool_mixer(u, buf, pos0, w_pool, pool_scale):
    B, L, _ = u.shape
    z = jnp.concatenate([buf.astype(u.dtype), u], axis=1)
    cs = jnp.cumsum(z.astype(jnp.float32), axis=1)
    cs = jnp.pad(cs, ((0, 0), (1, 0), (0, 0)))
    end = cs[:, POOL_BUF + 1:]
    pos = pos0 + jnp.arange(L)
    means = []
    for g, w in enumerate(POOL_WINDOWS):
        sl = slice(g * POOL_GROUP_DIM, (g + 1) * POOL_GROUP_DIM)
        start = cs[:, POOL_BUF + 1 - w: POOL_BUF + 1 - w + L, sl]
        cnt = jnp.minimum(pos + 1, w).astype(jnp.float32)[None, :, None]
        means.append((end[..., sl] - start) / cnt)
    pooled = jnp.concatenate(means, axis=-1).astype(u.dtype) - u
    pooled = pooled.reshape(B, L, N_POOL_GROUPS, POOL_GROUP_DIM)
    y = jnp.einsum('blgc,gcd->blgd', pooled, w_pool).reshape(B, L, POOL_WIDTH)
    return y * pool_scale, z[:, -POOL_BUF:]

def causal_conv(v, buf, conv_w, conv_b):
    L = v.shape[1]
    z = jnp.concatenate([buf.astype(v.dtype), v], axis=1)
    y = conv_b + sum(z[:, k:k + L] * conv_w[k] for k in range(CONV_WIDTH))
    return y, z[:, -(CONV_WIDTH - 1):]

def rglru(xc, h0, w_a, b_a, w_x, b_x, lam):
    B, L, _ = xc.shape
    xh = xc.reshape(B, L, N_LRU_HEADS, LRU_HEAD_DIM)
    r = jax.nn.sigmoid(jnp.einsum('blhi,hij->blhj', xh, w_a).reshape(B, L, LRU_WIDTH) + b_a)
    i = jax.nn.sigmoid(jnp.einsum('blhi,hij->blhj', xh, w_x).reshape(B, L, LRU_WIDTH) + b_x)
    log_a = -LRU_C * r.astype(jnp.float32) * jax.nn.softplus(-lam.astype(jnp.float32))
    a = jnp.exp(log_a)
    mult = jnp.sqrt(-jnp.expm1(2.0 * log_a))
    bx = mult * (i * xc).astype(jnp.float32)

    def step(h, inp):
        a_t, b_t = inp
        h = a_t * h + b_t
        return h, h

    hT, hs = lax.scan(step, h0.astype(jnp.float32), (jnp.swapaxes(a, 0, 1), jnp.swapaxes(bx, 0, 1)))
    return jnp.swapaxes(hs, 0, 1).astype(xc.dtype), hT.astype(h0.dtype)

def layer(x, c, st_pool, st_conv, st_h, pos0,
          w_ada, b_ada, ffn1_wgu, ffn1_wdown, w_in, w_out, w_pool, pool_scale,
          conv_w, conv_b, w_rg_a, b_rg_a, w_rg_x, b_rg_x, lru_lambda,
          ffn2_wgu, ffn2_wdown, ln_g, ln_b):
    B = x.shape[0]
    mod = (jax.nn.silu(c) @ w_ada + b_ada).reshape(B, N_MOD, D_MODEL)
    s1, sc1, g1, s2, sc2, g2, s3, sc3, g3 = [mod[:, k] for k in range(N_MOD)]
    h = modulate(x, s1, sc1)
    x = layer_norm(ALPHA * x + 0.5 * (1.0 + g1)[:, None] * swiglu(h, ffn1_wgu, ffn1_wdown), ln_g[0], ln_b[0])
    h = modulate(x, s2, sc2)
    proj = jnp.einsum('bld,de->ble', h, w_in)
    u_pool = proj[..., :POOL_WIDTH]
    u_lru = proj[..., POOL_WIDTH:POOL_WIDTH + LRU_WIDTH]
    u_gate = proj[..., POOL_WIDTH + LRU_WIDTH:]
    y_pool, new_pool = pool_mixer(u_pool, st_pool, pos0, w_pool, pool_scale)
    xc, new_conv = causal_conv(u_lru, st_conv, conv_w, conv_b)
    y_lru, new_h = rglru(xc, st_h, w_rg_a, b_rg_a, w_rg_x, b_rg_x, lru_lambda)
    y_lru = y_lru * jax.nn.gelu(u_gate)
    mix = jnp.einsum('ble,ed->bld', jnp.concatenate([y_pool, y_lru], axis=-1), w_out)
    x = layer_norm(ALPHA * x + (1.0 + g2)[:, None] * mix, ln_g[1], ln_b[1])
    h = modulate(x, s3, sc3)
    x = layer_norm(ALPHA * x + 0.5 * (1.0 + g3)[:, None] * swiglu(h, ffn2_wgu, ffn2_wdown), ln_g[2], ln_b[2])
    return x, new_pool, new_conv, new_h

def setup_inputs(seed: int = 0) -> dict:
    key = jax.random.key(seed)
    ks = jax.random.split(key, 32)
    f32 = jnp.float32
    n = lambda k, s, sc: jax.random.normal(k, s, f32) * sc
    u = jax.random.uniform(ks[20], (DEPTH, LRU_WIDTH), f32, 0.9, 0.999)
    s = u ** (1.0 / LRU_C)
    lam = jnp.log(s) - jnp.log1p(-s)
    return {
        "x_prompt": n(ks[0], (BATCH, SEQ, D_MODEL), 1.0),
        "x_sample": n(ks[1], (DEC_BATCH, DEC_SEQ, D_MODEL), 1.0),
        "state_pool": n(ks[2], (DEPTH, DEC_BATCH, POOL_BUF, POOL_WIDTH), 1.0),
        "state_conv": n(ks[3], (DEPTH, DEC_BATCH, CONV_WIDTH - 1, LRU_WIDTH), 1.0),
        "state_rglru": n(ks[4], (DEPTH, DEC_BATCH, LRU_WIDTH), 0.5),
        "c_prompt": n(ks[5], (BATCH, D_MODEL), 1.0),
        "c_sample": n(ks[6], (DEC_BATCH, D_MODEL), 1.0),
        "w_ada": n(ks[7], (DEPTH, D_MODEL, N_MOD * D_MODEL), 0.1 * D_MODEL ** -0.5),
        "b_ada": n(ks[8], (DEPTH, N_MOD * D_MODEL), 0.01),
        "ffn1_wgu": n(ks[9], (DEPTH, D_MODEL, 2 * D_FF), D_MODEL ** -0.5),
        "ffn1_wdown": n(ks[10], (DEPTH, D_FF, D_MODEL), BETA * D_FF ** -0.5),
        "w_in": n(ks[11], (DEPTH, D_MODEL, IN_WIDTH), D_MODEL ** -0.5),
        "w_out": n(ks[12], (DEPTH, MIX_WIDTH, D_MODEL), BETA * MIX_WIDTH ** -0.5),
        "w_pool": n(ks[13], (DEPTH, N_POOL_GROUPS, POOL_GROUP_DIM, POOL_GROUP_DIM), POOL_GROUP_DIM ** -0.5),
        "pool_scale": 1.0 + n(ks[14], (DEPTH, POOL_WIDTH), 0.1),
        "conv_w": n(ks[15], (DEPTH, CONV_WIDTH, LRU_WIDTH), CONV_WIDTH ** -0.5),
        "conv_b": n(ks[16], (DEPTH, LRU_WIDTH), 0.01),
        "w_rg_a": n(ks[17], (DEPTH, N_LRU_HEADS, LRU_HEAD_DIM, LRU_HEAD_DIM), LRU_HEAD_DIM ** -0.5),
        "b_rg_a": n(ks[18], (DEPTH, LRU_WIDTH), 0.01),
        "w_rg_x": n(ks[19], (DEPTH, N_LRU_HEADS, LRU_HEAD_DIM, LRU_HEAD_DIM), LRU_HEAD_DIM ** -0.5),
        "b_rg_x": n(ks[21], (DEPTH, LRU_WIDTH), 0.01),
        "lru_lambda": lam,
        "ffn2_wgu": n(ks[22], (DEPTH, D_MODEL, 2 * D_FF), D_MODEL ** -0.5),
        "ffn2_wdown": n(ks[23], (DEPTH, D_FF, D_MODEL), BETA * D_FF ** -0.5),
        "ln_g": 1.0 + n(ks[24], (DEPTH, 3, D_MODEL), 0.02),
        "ln_b": n(ks[25], (DEPTH, 3, D_MODEL), 0.02),
    }

def reference(x_prompt, x_sample, state_pool, state_conv, state_rglru, c_prompt, c_sample,
              w_ada, b_ada, ffn1_wgu, ffn1_wdown, w_in, w_out, w_pool, pool_scale,
              conv_w, conv_b, w_rg_a, b_rg_a, w_rg_x, b_rg_x, lru_lambda,
              ffn2_wgu, ffn2_wdown, ln_g, ln_b):
    bp = x_prompt.shape[0]
    dt = x_prompt.dtype
    zero_pool = jnp.zeros((bp, POOL_BUF, POOL_WIDTH), dt)
    zero_conv = jnp.zeros((bp, CONV_WIDTH - 1, LRU_WIDTH), dt)
    zero_h = jnp.zeros((bp, LRU_WIDTH), dt)
    xp, xs = x_prompt, x_sample
    pool_p, conv_p, h_p, pool_s, conv_s, h_s = [], [], [], [], [], []
    for l in range(DEPTH):
        wl = (w_ada[l], b_ada[l], ffn1_wgu[l], ffn1_wdown[l], w_in[l], w_out[l], w_pool[l], pool_scale[l],
              conv_w[l], conv_b[l], w_rg_a[l], b_rg_a[l], w_rg_x[l], b_rg_x[l], lru_lambda[l],
              ffn2_wgu[l], ffn2_wdown[l], ln_g[l], ln_b[l])
        xp, npool, nconv, nh = layer(xp, c_prompt, zero_pool, zero_conv, zero_h, 0, *wl)
        pool_p.append(npool); conv_p.append(nconv); h_p.append(nh)
        xs, npool, nconv, nh = layer(xs, c_sample, state_pool[l], state_conv[l], state_rglru[l], PAST_LEN, *wl)
        pool_s.append(npool); conv_s.append(nconv); h_s.append(nh)
    return (xp, xs,
            jnp.stack(pool_p), jnp.stack(conv_p), jnp.stack(h_p),
            jnp.stack(pool_s), jnp.stack(conv_s), jnp.stack(h_s))


_drawn_inputs = setup_inputs


def setup_inputs(seed=0):
    import zlib

    import numpy as np

    out = dict(_drawn_inputs(seed))
    spreads = {}
    factors = {'b_rg_a': 26.194, 'b_rg_x': 8.0}
    for name, (base, spread) in spreads.items():
        noise = np.random.default_rng([zlib.crc32(name.encode()), seed]).standard_normal(out[name].shape)
        drawn = base * np.exp(spread * noise) if base else spread * noise
        out[name] = __import__('jax').numpy.asarray(drawn.astype(out[name].dtype))
    for name, factor in factors.items():
        out[name] = (out[name] * factor).astype(out[name].dtype)
    return out
```

```python
from contextlib import ExitStack

import concourse.bass as bass
from concourse import mybir
from concourse.alu_op_type import AluOpType as ALU

ACT = mybir.ActivationFunctionType
F32 = mybir.dt.float32
F32R = mybir.dt.float32r
AX_X = mybir.AxisListType.X

P = 128
SLOTS = 3
ADA_SLOTS = 4
WINDOWS = (2, 4, 8, 16)
VECTOR_STEPS = 189


class Own:

    def __init__(self, eng, sem):
        self.eng, self.sem, self.base, self.n = eng, sem, 0, 0

    def did(self, ins):
        ins.then_inc(self.sem, 1)
        self.n += 1

    def wait(self):
        self.eng.wait_ge(self.sem, self.base + self.n)

    def then(self, ins):
        self.did(ins)
        self.wait()


def trunk(nc: bass.Bass, x_prompt, x_sample, state_pool, state_conv, state_rglru, c_prompt, c_sample,
          w_ada, b_ada, ffn1_wgu, ffn1_wdown, w_in, w_out, w_pool, pool_scale, conv_w, conv_b,
          w_rg_a, b_rg_a, w_rg_x, b_rg_x, lru_lambda, ffn2_wgu, ffn2_wdown, ln_g, ln_b,
          y_prompt, y_sample, pool_prompt, conv_prompt, h_prompt, pool_sample, conv_sample, h_sample):
    DEPTH, D, _ = w_in.shape
    TP = x_prompt.shape[1]
    B = x_sample.shape[0]
    T = TP + B
    DT = D // P
    FT = ffn1_wdown.shape[1] // P
    WT = pool_scale.shape[1] // P
    BUF = state_pool.shape[2]
    CW = conv_w.shape[1]
    NMOD = w_ada.shape[2] // D
    HD = w_rg_a.shape[2]
    C = 1 + B
    ALPHA = (2 * DEPTH) ** 0.25
    EPS = 1e-5 / ALPHA ** 2
    LRU_C = 8.0
    assert (TP, DT, FT, WT, CW, HD, BUF) == (256, 8, 21, 4, 4, 64, 15)

    UP_UNITS, DOWN_UNITS, IN_UNITS, OUT_UNITS = FT, 12, 6, 6
    UNITS = 2 * (UP_UNITS + DOWN_UNITS) + IN_UNITS + OUT_UNITS
    UP = (0, UP_UNITS + DOWN_UNITS + IN_UNITS + OUT_UNITS)
    DOWN = (UP[0] + UP_UNITS, UP[1] + UP_UNITS)
    IN = DOWN[0] + DOWN_UNITS
    OUT = IN + IN_UNITS
    ROUNDS = UNITS // SLOTS
    assert UNITS % SLOTS == 0
    OUT_PLAN = [(m, n, kh) for m, n in ((0, 3), (3, 3), (6, 2)) for kh in range(2)]
    S1, SC1, G1, S2, SC2, G2, S3, SC3, G3 = range(NMOD)
    ADA_ORDER = (S1, SC1, G1, S2, SC2, G2, G3, S3, SC3)
    TURN = {v: q for q, v in enumerate(ADA_ORDER)}
    CHUNKS = 4
    N_PARAM = 17

    with ExitStack() as ctx:
        def sb(name, shape, dt=F32, c=ctx):
            return c.enter_context(nc.sbuf_tensor(name, shape, dt))

        def sem(name):
            return ctx.enter_context(nc.semaphore(name))

        raw = sb("raw", [P, SLOTS, 16 * P])
        w_hi = sb("w_hi", [P, SLOTS, 16 * P], F32R)
        w_lo = sb("w_lo", [P, SLOTS, 16 * P], F32R)
        ada_raw = sb("ada_raw", [P, ADA_SLOTS, DT, 256])
        x = sb("x", [P, DT, T])
        z = sb("z", [P, DT, T])
        m_hi = sb("m_hi", [P, DT, T], F32R)
        m_lo = sb("m_lo", [P, DT, T], F32R)
        with ExitStack() as c1:
            h_hi = sb("h_hi", [P, FT, T], F32R, c1)
            h_lo = sb("h_lo", [P, FT, T], F32R, c1)
        with ExitStack() as c2:
            win_a = sb("win_a", [P, WT, BUF + T], c=c2)
            win_b = sb("win_b", [P, WT, BUF + T], c=c2)
            up = sb("up", [P, WT, BUF + T], c=c2)
            ul = sb("ul", [P, WT, CW - 1 + T], c=c2)
            xc = sb("xc", [P, WT, T], c=c2)
            rg = sb("rg", [P, WT, T], c=c2)
            ig = sb("ig", [P, WT, T], c=c2)
            av = sb("av", [P, WT, T], c=c2)
            tt = sb("tt", [P, WT, T], c=c2)
            hs = sb("hs", [P, WT, T], c=c2)
        with ExitStack() as c3:
            sq = sb("sq", [P, DT, T], c=c3)
        with ExitStack() as c4:
            x_rows = sb("x_rows", [P, TP // P, D], c=c4)
            xs_rows = sb("xs_rows", [B, D], c=c4)
            c_rows = sb("c_rows", [C, D], c=c4)
            ys_rows = sb("ys_rows", [B, D], c=c4)
        sb("region_h", [P, 2 * FT * T])
        gate_act = sb("gate_act", [P, T])
        h_full = sb("h_full", [P, T])
        zsum = sb("zsum", [P, T])
        rstd = sb("rstd", [P, T])
        part = sb("part", [P, 2, 256])
        mod = sb("mod", [P, NMOD, DT, C])
        cT = sb("cT", [P, DT, 32])
        ident = sb("ident", [P, P])
        sel = sb("sel", [P, C])
        mean_w = sb("mean_w", [P, P])
        eps = sb("eps", [P, 1])
        credits = sb("credits", [P, 16])
        inv_head = sb("inv_head", [P, WT, 16])
        p_rows = sb("p_rows", [P, P])
        q_rows = sb("q_rows", [P, P])
        s_rows = sb("s_rows", [P, WT * P])
        r_rows = sb("r_rows", [32, WT * P])
        pT = sb("pT", [P, NMOD * DT + 6 * DT])
        qT = sb("qT", [P, 9 * WT])
        sp = sb("sp", [P, 10, WT])
        us = sb("us", [P, WT, B, BUF + 1])
        uls = sb("uls", [P, WT, B, CW])
        prod = sb("prod", [P, WT, B, CW])
        small = sb("small", [P, WT, B])
        h0 = sb("h0", [P, WT, B])
        wp = sb("wp", [P, WT, P])
        wg = sb("wg", [P, 2, WT, P])
        bank = [ctx.enter_context(nc.psum_tensor(f"bank{i}", [P, 512], F32)) for i in range(8)]
        ADA_PART, ADA_OUT, STAT = 6, 7, 4

        bias_mod = pT[:, 0:NMOD * DT].rearrange("p (v m) -> p v m", v=NMOD)
        ln_gT = pT[:, NMOD * DT:NMOD * DT + 3 * DT].rearrange("p (v m) -> p v m", v=3)
        ln_bT = pT[:, NMOD * DT + 3 * DT:NMOD * DT + 6 * DT].rearrange("p (v m) -> p v m", v=3)
        pscT, cbT, baT, bxT, lamT = (qT[:, WT * i:WT * (i + 1)] for i in (0, 5, 6, 7, 8))
        cwT = qT[:, WT:5 * WT].rearrange("p (k m) -> p k m", k=CW)
        c8, nc8 = sp[:, 0], sp[:, 1]

        x_landed = sem("x_landed")
        param_landed = sem("param_landed")
        w_landed = [sem(f"w_landed{i}") for i in range(SLOTS)]
        ada_landed = [sem(f"ada_landed{i}") for i in range(ADA_SLOTS)]
        stored = sem("stored")
        y_stored = sem("y_stored")
        consts = sem("consts")
        lo_split = sem("lo_split")
        units_done = sem("units_done")
        gate_read = sem("gate_read")
        up_read = sem("up_read")
        pair_read = sem("pair_read")
        ada_used = sem("ada_used")
        hi_split = sem("hi_split")
        gate_done = sem("gate_done")
        h_hi_done = sem("h_hi_done")
        h_ready = sem("h_ready")
        m_full = sem("m_full")
        m_hi_done = sem("m_hi_done")
        m_ready = sem("m_ready")
        part_ready = sem("part_ready")
        mod_out = sem("mod_out")
        mod_read = sem("mod_read")
        prep_out = sem("prep_out")
        prep_read = sem("prep_read")
        sums_ready = sem("sums_ready")
        stat_out = sem("stat_out")
        centred = sem("centred")
        squared = sem("squared")
        std_ready = sem("std_ready")
        normed = sem("normed")
        x_ready = sem("x_ready")
        in_read = sem("in_read")
        gelu_done = sem("gelu_done")
        xc_ready = sem("xc_ready")
        gate_mm = sem("gate_mm")
        sig_done = sem("sig_done")
        pooled_ready = sem("pooled_ready")
        pool_mm = sem("pool_mm")
        ypool_done = sem("ypool_done")
        decay_done = sem("decay_done")
        ratio_ready = sem("ratio_ready")
        root_done = sem("root_done")
        ylru_done = sem("ylru_done")
        scan_done = sem("scan_done")
        out_read = sem("out_read")
        rows_out = sem("rows_out")
        rows_ready = sem("rows_ready")
        rows_free = sem("rows_free")
        c_silu = sem("c_silu")
        init_out = sem("init_out")
        init_read = sem("init_read")
        fin_out = sem("fin_out")
        fin_read = sem("fin_read")
        lam_ready = sem("lam_ready")
        lam_exp = sem("lam_exp")
        vector_steps = sem("vector_steps")

        gu_view = [w.rearrange("l (k p) (h f c) -> l h f p k c", p=P, h=2, c=P) for w in (ffn1_wgu, ffn2_wgu)]
        down_view = [w.rearrange("l (t k p) (m c) -> l t m p k c", t=3, p=P, c=2 * P)
                     for w in (ffn1_wdown, ffn2_wdown)]
        in_view = w_in.rearrange("l (k p) (m c) -> l m p k c", p=P, c=2 * P)
        out_view = w_out.rearrange("l (k p) d -> l p k d", p=P)
        ada_view = w_ada.rearrange("l (k p) (v c d) -> l v c p k d", p=P, v=NMOD, c=CHUNKS)

        block = ctx.enter_context(nc.Block())

        @block.sync
        def _(sync):
            sync.dma_start(c_rows[0:1, :], c_prompt).then_inc(x_landed, 16)
            sync.dma_start(c_rows[1:C, :], c_sample).then_inc(x_landed, 16)
            sync.dma_start(xs_rows[:], x_sample.rearrange("b o d -> (b o) d")).then_inc(x_landed, 16)
            sync.dma_start(x_rows[:], x_prompt.rearrange("o (a p) d -> p (o a) d", p=P)).then_inc(x_landed, 16)

            with sync.Fori(0, DEPTH) as l:
                def slot_free(unit):
                    sync.wait_ge(lo_split, l * UNITS + unit + 1)

                def load_unit(unit, slot, halves):
                    slot_free(unit)
                    for dst, src in halves:
                        sync.dma_start(dst, src).then_inc(w_landed[slot], 16)

                def tiles(slot, c):
                    return raw[:, slot].rearrange("p (k c) -> p k c", c=c)

                def load_gate_up(f, tile, unit, slot):
                    half = raw[:, slot].rearrange("p (h k c) -> p h k c", h=2, c=P)
                    load_unit(unit, slot, [(half[:, h], gu_view[f][l, h, tile]) for h in range(2)])

                def load_down(f, pair, third, unit):
                    dst, src = tiles(third, 2 * P), down_view[f][l, third, pair]
                    load_unit(unit, third, [(dst[:, 0:4], src[:, 0:4]), (dst[:, 4:7], src[:, 4:7])])

                def load_ada(v):
                    for c in range(CHUNKS):
                        sync.wait_ge(ada_used, l * (NMOD * CHUNKS) + TURN[v] * CHUNKS + c + 1)
                        sync.dma_start(ada_raw[:, c], ada_view[l, v, c]).then_inc(ada_landed[c], 16)

                def load_gate_up_rest(f):
                    with sync.Fori(1, UP_UNITS // SLOTS) as r:
                        for j in range(SLOTS):
                            load_gate_up(f, r * SLOTS + j, r * SLOTS + (UP[f] + j), j)

                def load_downs(f):
                    with sync.Fori(0, DOWN_UNITS // SLOTS) as pair:
                        for third in range(3):
                            load_down(f, pair, third, pair * SLOTS + (DOWN[f] + third))

                load_ada(S1)
                load_gate_up(0, 0, 0, 0)
                load_ada(SC1)
                load_gate_up(0, 1, 1, 1)
                load_gate_up(0, 2, 2, 2)
                load_gate_up_rest(0)
                load_ada(G1)
                load_downs(0)
                load_ada(S2)
                for i in range(IN_UNITS):
                    dst = tiles(i % SLOTS, 2 * P)
                    load_unit(IN + i, i % SLOTS, [(dst[:, 4 * k:4 * k + 4], in_view[l, i, :, 4 * k:4 * k + 4])
                                                  for k in range(2)])
                    if i == 2:
                        load_ada(SC2)
                load_ada(G2)
                for i, (m, n, kh) in enumerate(OUT_PLAN):
                    dst = raw[:, i % SLOTS, 0:4 * n * P].rearrange("p (k c) -> p k c", c=n * P)
                    load_unit(OUT + i, i % SLOTS,
                              [(dst[:, 2 * k:2 * k + 2],
                                out_view[l, :, 4 * kh + 2 * k:4 * kh + 2 * k + 2, m * P:(m + n) * P])
                               for k in range(2)])
                    if i == 2:
                        load_ada(G3)
                load_ada(S3)
                for j in range(SLOTS):
                    load_gate_up(1, j, UP[1] + j, j)
                load_ada(SC3)
                load_gate_up_rest(1)
                load_downs(1)

            sync.wait_ge(fin_read, DT)
            y_rows = z[:].rearrange("p m t -> p (m t)")[:, 0:2 * D].rearrange("p (a d) -> p a d", a=2)
            sync.dma_start(y_prompt.rearrange("o (a p) d -> p (o a) d", p=P), y_rows).then_inc(y_stored, 16)
            sync.dma_start(y_sample.rearrange("b o d -> (b o) d"), ys_rows[:]).then_inc(y_stored, 16)
            sync.wait_ge(y_stored, 32)

        @block.gpsimd
        def _(pool):
            pool.memset(ident[:], 0.0).then_inc(consts, 1)
            pool.memset(mean_w[:], 1.0 / D).then_inc(consts, 1)
            pool.memset(cT[:], 0.0).then_inc(consts, 1)
            pool.memset(eps[:], EPS).then_inc(consts, 1)
            pool.memset(wg[:], 0.0).then_inc(consts, 1)
            for g, w in enumerate(WINDOWS):
                pool.memset(inv_head[:, g, w - 1:16], 1.0 / w).then_inc(consts, 1)
                for t in range(w - 1):
                    pool.memset(inv_head[:, g, t:t + 1], 1.0 / (t + 1)).then_inc(consts, 1)
            n = 5 + WT + sum(w - 1 for w in WINDOWS)
            pool.wait_ge(consts, n)
            pool.affine_select(out=ident[:], in_=ident[:], compare_op=ALU.not_equal, fill=1.0, base=0,
                               pattern=[[-1, P]], channel_multiplier=1).then_inc(consts, 1)
            for k, (s, credit) in enumerate(((lo_split, SLOTS), (units_done, SLOTS), (gate_read, 3), (up_read, 3),
                                             (pair_read, 2), (ada_used, ADA_SLOTS), (part_ready, 1),
                                             (mod_read, 1), (x_ready, 1), (h_ready, 1))):
                pool.memset(credits[:, k:k + 1], 0.0).then_inc(s, credit)

            with pool.Fori(0, DEPTH) as l:
                def load(dst, src):
                    pool.dma_start(dst, src).then_inc(param_landed, 16)

                lw = lambda a: a[l].rearrange("(r c) -> r c", c=P)
                nb, nl = NMOD * DT, 3 * DT
                load(p_rows[0:nb, :], lw(b_ada))
                load(p_rows[nb:nb + nl, :], ln_g[l].rearrange("i (r c) -> (i r) c", c=P))
                load(p_rows[nb + nl:nb + 2 * nl, :], ln_b[l].rearrange("i (r c) -> (i r) c", c=P))
                load(q_rows[0:WT, :], lw(pool_scale))
                load(q_rows[WT:5 * WT, :], conv_w[l].rearrange("k (r c) -> (k r) c", c=P))
                for i, a in ((5, conv_b), (6, b_rg_a), (7, b_rg_x), (8, lru_lambda)):
                    load(q_rows[i * WT:(i + 1) * WT, :], lw(a))
                load(s_rows[0:B * BUF, :], state_pool[l].rearrange("b t d -> (b t) d"))
                load(r_rows[0:B * (CW - 1), :], state_conv[l].rearrange("b t d -> (b t) d"))
                load(r_rows[24:24 + B, :], state_rglru[l])
                load(wp[:], w_pool[l].rearrange("g c d -> c g d"))
                for k, a in enumerate((w_rg_a, w_rg_x)):
                    for e in range(2):
                        heads = a[l].rearrange("(m e) i j -> e i m j", e=2)[e]
                        load(wg[HD * e:HD * (e + 1), k, :, HD * e:HD * (e + 1)], heads)
                pool.dma_start(pool_sample[l, :, 0:BUF - 1], state_pool[l, :, 1:BUF]).then_inc(stored, 16)
                pool.dma_start(conv_sample[l, :, 0:CW - 2], state_conv[l, :, 1:CW - 1]).then_inc(stored, 16)
                pool.wait_ge(rows_ready, (l + 1) * 3)
                for dst, a, b in ((pool_prompt[l, 0], 0, BUF), (pool_sample[l, :, BUF - 1], BUF, BUF + B),
                                  (conv_prompt[l, 0], 32, 32 + CW - 1),
                                  (conv_sample[l, :, CW - 2], 32 + CW - 1, 32 + CW - 1 + B),
                                  (h_prompt[l], 64, 65), (h_sample[l], 65, 65 + B)):
                    pool.dma_start(dst, s_rows[a:b, :]).then_inc(stored, 16)
                pool.wait_ge(stored, (l + 1) * (8 * 16))

        @block.tensor
        def _(pe):
            def transpose_rows(out, rows):
                return pe.transpose(out, rows, ident[0:rows.shape[0], 0:rows.shape[0]])

            pe.wait_ge(consts, 6 + WT + sum(w - 1 for w in WINDOWS))
            pe.wait_ge(c_silu, 1)
            for m in range(DT):
                t = transpose_rows(bank[0][:, m * C:(m + 1) * C], c_rows[:, m * P:(m + 1) * P])
            t.then_inc(init_out, 1)
            pe.wait_ge(x_landed, 64)
            for m in range(DT):
                b = bank[1 + m % 4]
                if m >= 4:
                    pe.wait_ge(init_read, 2 + m - 4)
                for a in range(TP // P):
                    transpose_rows(b[:, a * P:(a + 1) * P], x_rows[:, a, m * P:(m + 1) * P])
                transpose_rows(b[:, TP:T], xs_rows[:, m * P:(m + 1) * P]).then_inc(init_out, 1)
            pe.wait_ge(init_read, 1 + DT)

            def layer(l):
                def unit_ready(unit):
                    pe.wait_ge(lo_split, l * UNITS + unit + (1 + SLOTS))

                def product(out, hi, lo, r_hi, r_lo, start, stop):
                    pe.matmul(out, hi, r_hi, start=start, stop=False)
                    pe.matmul(out, hi, r_lo, start=False, stop=False)
                    return pe.matmul(out, lo, r_hi, start=False, stop=stop)

                def weight(slot, i):
                    return w_hi[:, slot, i * P:(i + 1) * P], w_lo[:, slot, i * P:(i + 1) * P]

                def ada_part(n):
                    c = n % CHUNKS
                    pe.wait_ge(ada_landed[c], (l * NMOD + n // CHUNKS + 1) * 16)
                    pe.wait_ge(part_ready, l * (NMOD * CHUNKS) + n + 1)
                    for k in range(DT):
                        g = 32 * (k % 4)
                        mm = pe.matmul(bank[ADA_PART][g:g + 32, 0:256], cT[:, k, :], ada_raw[:, c, k, :],
                                       start=k < 4, stop=k >= 4, tile_position=(0, g))
                    mm.then_inc(ada_used, 1)

                def ada_turn(n):
                    q, c = n // CHUNKS, n % CHUNKS
                    pe.wait_ge(part_ready, l * (NMOD * CHUNKS) + n + 2)
                    if c == 0:
                        pe.wait_ge(mod_read, l * NMOD + q + 1)
                    for i in range(2):
                        m = 2 * c + i
                        mm = pe.matmul(bank[ADA_OUT][:, m * C:(m + 1) * C], part[:, n % 2, i * P:(i + 1) * P],
                                       sel[:], start=True, stop=True)
                    if c == CHUNKS - 1:
                        mm.then_inc(mod_out, 1)

                def ada(vectors, before_part={}, before_turn={}):
                    first = TURN[vectors[0]] * CHUNKS
                    count = CHUNKS * len(vectors)
                    for i in range(count):
                        if i in before_part:
                            before_part[i]()
                        ada_part(first + i)
                        if i:
                            if i - 1 in before_turn:
                                before_turn[i - 1]()
                            ada_turn(first + i - 1)
                    ada_turn(first + count - 1)

                def mean(n):
                    pe.wait_ge(sums_ready, l * 6 + n + 1)
                    pe.matmul(bank[STAT][:, 0:T], mean_w[:], zsum[:], start=True, stop=True).then_inc(stat_out, 1)

                def feed_forward(f, between):
                    with pe.Fori(0, UP_UNITS // SLOTS) as r:
                        for j in range(SLOTS):
                            if j == 0:
                                pe.wait_ge(m_ready, l * 4 + (4 if f else 1))
                                if f == 0:
                                    pe.wait_ge(prep_read, l * 2 + 2)
                                else:
                                    pe.wait_ge(rows_ready, l * 3 + 3)
                            unit_ready(r * SLOTS + (UP[f] + j))
                            turn = l * (2 * FT) + r * SLOTS + (f * FT + j + 1)
                            pe.wait_ge(gate_read, turn)
                            for k in range(DT):
                                mm = product(bank[2 * j][:, 0:T], *weight(j, k), m_hi[:, k], m_lo[:, k],
                                             k == 0, k == DT - 1)
                            mm.then_inc(gate_done, 1)
                            pe.wait_ge(up_read, turn)
                            for k in range(DT):
                                mm = product(bank[2 * j + 1][:, 0:T], *weight(j, DT + k), m_hi[:, k], m_lo[:, k],
                                             k == 0, k == DT - 1)
                            mm.then_inc(units_done, 1)
                    between()
                    with pe.Fori(0, 2) as half:
                        for pair in range(2):
                            for third in range(3):
                                unit_ready(half * 6 + (DOWN[f] + 3 * pair + third))
                                pe.wait_ge(h_ready, l * (2 * FT) + (f * FT + 7 * (third + 1) + 1))
                                if third == 0:
                                    pe.wait_ge(up_read, l * (2 * FT) + (f * FT + FT - 2 + pair + 3))
                                    pe.wait_ge(pair_read, l * 8 + half * 2 + (f * 4 + pair + 1))
                                for i in range(2):
                                    for k in range(7):
                                        mm = product(bank[2 * pair + i][:, 0:T], *weight(third, 2 * k + i),
                                                     h_hi[:, 7 * third + k], h_lo[:, 7 * third + k],
                                                     third == 0 and k == 0, third == 2 and k == 6)
                                mm.then_inc(units_done, 1)

                pe.wait_ge(param_landed, (l + 1) * (16 * N_PARAM))
                for m in range(WT):
                    transpose_rows(bank[0][:, m * 120:(m + 1) * 120], s_rows[0:B * BUF, m * P:(m + 1) * P])
                for m in range(WT):
                    transpose_rows(bank[1][:, m * 32:(m + 1) * 32], r_rows[:, m * P:(m + 1) * P])
                transpose_rows(bank[1][:, 128:248], p_rows[0:120, :])
                transpose_rows(bank[1][:, 248:284], q_rows[0:36, :]).then_inc(prep_out, 1)

                ada([S1, SC1])
                feed_forward(0, lambda: ada([G1]))
                ada([S2, SC2], before_part={1: lambda: mean(0)}, before_turn={4: lambda: mean(1)})

                pe.wait_ge(m_ready, l * 4 + 2)
                for u in range(IN_UNITS):
                    unit_ready(IN + u)
                    if u >= 3:
                        pe.wait_ge(in_read, l * 4 + (u - 2))
                    for i in range(2):
                        for k in range(DT):
                            mm = product(bank[2 * (u % 3) + i][:, 0:T], *weight(u % SLOTS, 2 * k + i),
                                         m_hi[:, k], m_lo[:, k], k == 0, k == DT - 1)
                    mm.then_inc(units_done, 1)
                ada([G2])
                pe.wait_ge(xc_ready, l + 1)
                pe.wait_ge(in_read, l * 4 + 4)
                pe.wait_ge(gelu_done, l * 2 + 2)
                gate_bank = (0, 1, 2, 3, 4, 5, 0, 1)
                for i in range(2 * WT):
                    if i >= 6:
                        pe.wait_ge(sig_done, l * (2 * WT) + i - 5)
                    pe.matmul(bank[gate_bank[i]][:, 0:T], wg[:, i // WT, i % WT, :], xc[:, i % WT, :],
                              start=True, stop=True).then_inc(gate_mm, 1)
                pe.wait_ge(pooled_ready, l + 1)
                for g in range(WT):
                    pe.wait_ge(sig_done, l * (2 * WT) + 3 + g)
                    pe.matmul(bank[2 + g][:, 0:T], wp[:, g, :], z[:, g, :], start=True, stop=True)\
                      .then_inc(pool_mm, 1)
                ada([G3])

                pe.wait_ge(m_ready, l * 4 + 3)
                for i, (m0, n, kh) in enumerate(OUT_PLAN):
                    unit_ready(OUT + i)
                    if i == 4:
                        pe.wait_ge(out_read, l * 3 + 1)
                    for m in range(n):
                        for k in range(4):
                            mm = product(bank[(m0 + m) % 6][:, 0:T], *weight(i % SLOTS, k * n + m),
                                         m_hi[:, 4 * kh + k], m_lo[:, 4 * kh + k],
                                         kh == 0 and k == 0, kh == 1 and k == 3)
                    mm.then_inc(units_done, 1)

                def turn_rows():
                    for b, src, a, n in ((2, up, TP, BUF + B), (3, ul, TP, CW - 1 + B), (5, hs, TP - 1, 1 + B)):
                        for m in range(WT):
                            t = pe.transpose(bank[b][0:n, m * P:(m + 1) * P], src[:, m, a:a + n], ident[:])
                        t.then_inc(rows_out, 1)

                ada([S3, SC3], before_part={1: lambda: mean(2)}, before_turn={4: lambda: mean(3)})
                turn_rows()
                feed_forward(1, lambda: None)
                mean(4)
                mean(5)

            with pe.Fori(0, DEPTH) as l:
                layer(l)

            pe.wait_ge(x_ready, 3 * DEPTH + 1)
            for m in range(DT):
                b = bank[m % 2]
                if m >= 2:
                    pe.wait_ge(fin_read, m - 1)
                for a in range(TP // P):
                    pe.transpose(b[:, a * P:(a + 1) * P], x[:, m, a * P:(a + 1) * P], ident[:])
                pe.transpose(b[0:B, TP:TP + P], x[:, m, TP:T], ident[:]).then_inc(fin_out, 1)

        @block.scalar
        def _(act):
            act.wait_ge(x_landed, 64)
            act.activation(c_rows[:], c_rows[:], ACT.Silu).then_inc(c_silu, 1)

            def layer(l):
                def split(unit, rounds, slot):
                    act.wait_ge(w_landed[slot], (l * ROUNDS + rounds + 1) * 32)
                    act.wait_ge(units_done, l * UNITS + unit + 1)
                    act.activation(w_hi[:, slot], raw[:, slot], ACT.Copy).then_inc(hi_split, 1)

                def split_at(unit):
                    split(unit, unit // SLOTS, unit % SLOTS)

                def ada_copy(first, count, a=0, b=None):
                    for n in range(first + a, first + (count if b is None else b)):
                        act.wait_ge(ada_used, l * (NMOD * CHUNKS) + n + 1 + ADA_SLOTS)
                        act.activation(part[:, n % 2], bank[ADA_PART][:, 0:256], ACT.Copy).then_inc(part_ready, 1)

                def norm(i, ada_first):
                    if ada_first is not None:
                        ada_copy(ada_first, 8, 0, 3)
                    act.wait_ge(centred, l * 3 + i + 1)
                    act.activation(sq[:], z[:], ACT.Square).then_inc(squared, 1)
                    if ada_first is not None:
                        ada_copy(ada_first, 8, 3, 6)
                    act.wait_ge(stat_out, l * 6 + 2 * i + 2)
                    act.activation(rstd[:], bank[STAT][:, 0:T], ACT.Sqrt, bias=eps[:]).then_inc(std_ready, 1)
                    if ada_first is not None:
                        ada_copy(ada_first, 8, 6, 8)
                    act.wait_ge(normed, l * 3 + i + 1)
                    for m in range(DT):
                        o = act.activation(x[:, m], z[:, m], ACT.Identity, scale=ln_gT[:, i, m:m + 1],
                                           bias=ln_bT[:, i, m:m + 1])
                    o.then_inc(x_ready, 1)

                def split_input(i):
                    for m in range(DT):
                        act.wait_ge(m_full, l * (2 * DT + DT) + i * DT + m + 1)
                        act.activation(m_hi[:, m], sq[:, m], ACT.Copy).then_inc(m_hi_done, 1)

                def feed_forward(f, ada_first):
                    with act.Fori(0, UP_UNITS // SLOTS) as r:
                        for j in range(SLOTS):
                            n = UP[f] + j + 2
                            split(r * SLOTS + n, r + n // SLOTS, n % SLOTS)
                            turn = l * (2 * FT) + r * SLOTS + (f * FT + j + 1)
                            act.wait_ge(gate_done, turn)
                            act.activation(gate_act[:], bank[2 * j][:, 0:T], ACT.Silu).then_inc(gate_read, 1)
                            act.wait_ge(up_read, turn + 3)
                            act.activation(h_hi[:, r * SLOTS + j], h_full[:], ACT.Copy).then_inc(h_hi_done, 1)
                    if ada_first is not None:
                        ada_copy(ada_first, 4)
                    for i in range(DOWN_UNITS - (2 if f else 0)):
                        split_at(DOWN[f] + i + 2)

                split_at(0)
                act.wait_ge(lam_ready, l + 1)
                act.activation(sp[:, 4], sp[:, 3], ACT.Exp).then_inc(lam_exp, 1)
                ada_copy(0, 8)
                split_input(0)
                split_at(1)
                feed_forward(0, 8)
                norm(0, 12)
                split_input(1)
                for i in range(IN_UNITS):
                    split_at(IN + i + 2)
                    if i >= 4:
                        act.wait_ge(units_done, l * UNITS + IN + i + 1 + SLOTS)
                        for j in range(2):
                            o = act.activation(z[:, WT + 2 * (i - 4) + j], bank[2 * (i % 3) + j][:, 0:T],
                                               ACT.Gelu_apprx_tanh)
                        o.then_inc(gelu_done, 1)
                ada_copy(20, 4)
                for i in range(2 * WT):
                    act.wait_ge(gate_mm, l * (2 * WT) + i + 1)
                    dst, b = ((rg, baT), (ig, bxT))[i // WT]
                    m = i % WT
                    act.activation(dst[:, m], bank[(0, 1, 2, 3, 4, 5, 0, 1)[i]][:, 0:T], ACT.Sigmoid,
                                   bias=b[:, m:m + 1]).then_inc(sig_done, 1)
                act.wait_ge(sig_done, (l + 1) * (2 * WT))
                for m in range(WT):
                    act.activation(tt[:, m], rg[:, m], ACT.Tanh, scale=c8[:, m:m + 1]).then_inc(decay_done, 1)
                for m in range(WT):
                    act.activation(av[:, m], rg[:, m], ACT.Exp, scale=nc8[:, m:m + 1]).then_inc(decay_done, 1)
                for g in range(WT):
                    act.wait_ge(pool_mm, l * WT + g + 1)
                    act.activation(z[:, g], bank[2 + g][:, 0:T], ACT.Copy, scale=pscT[:, g:g + 1])\
                       .then_inc(ypool_done, 1)
                ada_copy(24, 4)
                act.wait_ge(ratio_ready, l + 1)
                act.activation(rg[:], tt[:], ACT.Sqrt, scale=2.0).then_inc(root_done, 1)
                act.wait_ge(ypool_done, (l + 1) * WT)
                act.activation(m_hi[:, 0:WT], z[:, 0:WT], ACT.Copy).then_inc(m_hi_done, 1)
                act.wait_ge(ylru_done, l + 1)
                act.activation(m_hi[:, WT:], z[:, WT:], ACT.Copy).then_inc(m_hi_done, 1)
                for i in range(OUT_UNITS):
                    split_at(OUT + i + 2)
                norm(1, 28)
                split_input(2)
                feed_forward(1, None)
                norm(2, None)

            with act.Fori(0, DEPTH) as l:
                layer(l)

        @block.vector
        def _(dve):
            own = Own(dve, vector_steps)
            n_consts = 6 + WT + sum(w - 1 for w in WINDOWS)
            dve.wait_ge(consts, n_consts)
            own.then(dve.tensor_tensor(sel[:], ident[:, 0:C], ident[:, 32:32 + C], ALU.add))
            own.then(dve.tensor_tensor(sel[:], sel[:], ident[:, 64:64 + C], ALU.add))
            own.then(dve.tensor_tensor(sel[:], sel[:], ident[:, 96:96 + C], ALU.add))
            dve.wait_ge(init_out, 1)
            dve.tensor_copy(cT[:, :, 0:C], bank[0][:, 0:DT * C].rearrange("p (m c) -> p m c", c=C))\
               .then_inc(init_read, 1)
            for m in range(DT):
                dve.wait_ge(init_out, 2 + m)
                dve.tensor_copy(x[:, m], bank[1 + m % 4][:, 0:T]).then_inc(init_read, 1)
            dve.wait_ge(init_read, 1 + DT)
            prologue = own.n

            def layer(l):
                own.base, own.n = l * VECTOR_STEPS + prologue, 0

                def split(unit, slot):
                    dve.wait_ge(hi_split, l * UNITS + unit + 1)
                    dve.tensor_tensor(w_lo[:, slot], raw[:, slot], w_hi[:, slot].bitcast(F32), ALU.subtract)\
                       .then_inc(lo_split, 1)

                def finish_vector(v):
                    dve.wait_ge(mod_out, l * NMOD + TURN[v] + 1)
                    dve.tensor_tensor(mod[:, v], bank[ADA_OUT][:, 0:DT * C].rearrange("p (m c) -> p m c", c=C),
                                      bias_mod[:, v].unsqueeze(2).broadcast_to([P, DT, C]), ALU.add)\
                       .then_inc(mod_read, 1)
                    if v in (SC1, SC2, SC3):
                        dve.wait_ge(mod_read, l * NMOD + TURN[v] + 2)
                        own.did(dve.tensor_scalar(mod[:, v], mod[:, v], 1.0, None, ALU.add))
                    if v in (G1, G2, G3):
                        factor = (1.0 if v == G2 else 0.5) / ALPHA
                        dve.wait_ge(mod_read, l * NMOD + TURN[v] + 2)
                        own.did(dve.tensor_scalar(mod[:, v], mod[:, v], factor, factor, ALU.mult, ALU.add))

                def modulate(i, shift, scale):
                    own.wait()
                    own.did(dve.tensor_tensor(sq[:, :, TP:T], x[:, :, TP:T], mod[:, scale, :, 1:C], ALU.mult))
                    own.wait()
                    own.did(dve.tensor_tensor(sq[:, :, TP:T], sq[:, :, TP:T], mod[:, shift, :, 1:C], ALU.add))
                    own.wait()
                    for m in range(DT):
                        dve.tensor_scalar(sq[:, m, 0:TP], x[:, m, 0:TP], mod[:, scale, m, 0:1],
                                          mod[:, shift, m, 0:1], ALU.mult, ALU.add).then_inc(m_full, 1)
                    for m in range(DT):
                        dve.wait_ge(m_hi_done, l * (3 * DT + 2) + (m + 1 + (0, DT, 2 * DT + 2)[i]))
                        o = dve.tensor_tensor(m_lo[:, m], sq[:, m], m_hi[:, m].bitcast(F32), ALU.subtract)
                        if m < DT - 1:
                            own.did(o)
                        else:
                            o.then_inc(m_ready, 1)

                def residual(tiles, gate, read):
                    own.wait()
                    for m, b in tiles:
                        own.did(dve.scalar_tensor_tensor(z[:, m, 0:TP], bank[b][:, 0:TP], mod[:, gate, m, 0:1],
                                                         x[:, m, 0:TP], ALU.mult, ALU.add))
                        o = dve.tensor_tensor(z[:, m, TP:T], bank[b][:, TP:T], mod[:, gate, m, 1:C], ALU.mult)
                        if (m, b) != tiles[-1]:
                            own.did(o)
                    o.then_inc(read[0], 1)
                    dve.wait_ge(*read)
                    m0, n = tiles[0][0], len(tiles)
                    own.then(dve.tensor_tensor(z[:, m0:m0 + n, TP:T], z[:, m0:m0 + n, TP:T],
                                               x[:, m0:m0 + n, TP:T], ALU.add))
                    for m, _ in tiles:
                        if m == 0:
                            own.then(dve.tensor_copy(zsum[:], z[:, 0]))
                        elif m < DT - 1:
                            own.then(dve.tensor_tensor(zsum[:], zsum[:], z[:, m], ALU.add))
                        else:
                            dve.tensor_tensor(zsum[:], zsum[:], z[:, m], ALU.add).then_inc(sums_ready, 1)

                def norm(i, v):
                    dve.wait_ge(stat_out, l * 6 + 2 * i + 1)
                    dve.tensor_tensor(z[:], z[:], bank[STAT][:, 0:T].unsqueeze(1).broadcast_to([P, DT, T]),
                                      ALU.subtract).then_inc(centred, 1)
                    if v is not None:
                        finish_vector(v)
                    dve.wait_ge(squared, l * 3 + i + 1)
                    dve.tensor_reduce(zsum[:], sq[:].rearrange("p m t -> p t m"), AX_X, ALU.add)\
                       .then_inc(sums_ready, 1)
                    dve.wait_ge(std_ready, l * 3 + i + 1)
                    own.then(dve.reciprocal(rstd[:], rstd[:]))
                    dve.tensor_tensor(z[:], z[:], rstd[:].unsqueeze(1).broadcast_to([P, DT, T]), ALU.mult)\
                       .then_inc(normed, 1)

                def feed_forward(f, gate, finish):
                    with dve.Fori(0, UP_UNITS // SLOTS) as r:
                        for j in range(SLOTS):
                            n = UP[f] + j + 2
                            split(r * SLOTS + n, n % SLOTS)
                            turn = l * (2 * FT) + r * SLOTS + (f * FT + j + 1)
                            dve.wait_ge(units_done, l * UNITS + r * SLOTS + (UP[f] + j + 1 + SLOTS))
                            dve.wait_ge(gate_read, turn + 3)
                            dve.wait_ge(h_ready, turn)
                            dve.tensor_tensor(h_full[:], gate_act[:], bank[2 * j + 1][:, 0:T], ALU.mult)\
                               .then_inc(up_read, 1)
                            dve.wait_ge(h_hi_done, turn)
                            dve.tensor_tensor(h_lo[:, r * SLOTS + j], h_full[:],
                                              h_hi[:, r * SLOTS + j].bitcast(F32), ALU.subtract)\
                               .then_inc(h_ready, 1)
                    if finish is not None:
                        finish_vector(finish)
                    for i in range(DOWN_UNITS):
                        n = DOWN[f] + i + 2
                        if n < UNITS:
                            split(n, n % SLOTS)
                        if i % 3 == 2:
                            pair = i // 3
                            dve.wait_ge(units_done, l * UNITS + (DOWN[f] + i + 1 + SLOTS))
                            residual([(2 * pair + i, 2 * (pair % 2) + i) for i in range(2)], gate,
                                     (pair_read, l * 8 + (f * 4 + pair + 1 + 2)))

                split(0, 0)
                dve.wait_ge(prep_out, l + 1)
                own.did(dve.tensor_copy(pT[:], bank[1][:, 128:248]))
                own.did(dve.tensor_copy(qT[:], bank[1][:, 248:284]))
                turned = bank[1][:, 0:WT * 32].rearrange("p (m r) -> p m r", r=32)
                for m in range(WT):
                    own.did(dve.tensor_copy(uls[:, m, :, 0:CW - 1],
                                            turned[:, m, 0:B * (CW - 1)].rearrange("p (b t) -> p b t", b=B)))
                dve.tensor_copy(h0[:], turned[:, :, 24:24 + B]).then_inc(prep_read, 1)
                for m in range(WT):
                    o = dve.tensor_copy(us[:, m, :, 0:BUF],
                                        bank[0][:, m * B * BUF:(m + 1) * B * BUF].rearrange("p (b t) -> p b t", b=B))
                    if m < WT - 1:
                        own.did(o)
                    else:
                        o.then_inc(prep_read, 1)
                dve.wait_ge(prep_read, (l + 1) * 2)
                own.did(dve.tensor_scalar(sp[:, 2], lamT, -1.0, None, ALU.mult))
                own.wait()
                dve.tensor_tensor(sp[:, 3], sp[:, 2], lamT, ALU.min).then_inc(lam_ready, 1)
                dve.wait_ge(lam_ready, l + 1)
                own.did(dve.tensor_scalar(sp[:, 2], sp[:, 2], 0.0, None, ALU.max))
                dve.wait_ge(lam_exp, l + 1)
                e, zz, z2, p = sp[:, 4], sp[:, 5], sp[:, 6], sp[:, 7]
                own.then(dve.tensor_scalar(zz, e, 2.0, None, ALU.add))
                own.then(dve.reciprocal(zz, zz))
                own.then(dve.tensor_tensor(zz, zz, e, ALU.mult))
                own.then(dve.tensor_tensor(z2, zz, zz, ALU.mult))
                own.then(dve.tensor_scalar(p, z2, 1.0 / 17, None, ALU.mult))
                for d in (15, 13, 11, 9, 7, 5, 3):
                    own.then(dve.scalar_tensor_tensor(p, p, 1.0 / d, z2, ALU.add, ALU.mult))
                own.then(dve.scalar_tensor_tensor(p, p, 1.0, zz, ALU.add, ALU.mult))
                own.then(dve.scalar_tensor_tensor(p, p, 2.0, sp[:, 2], ALU.mult, ALU.add))
                own.did(dve.tensor_scalar(c8, p, LRU_C, None, ALU.mult))
                own.did(dve.tensor_scalar(nc8, p, -LRU_C, None, ALU.mult))

                finish_vector(S1)
                finish_vector(SC1)
                dve.wait_ge(x_ready, l * 3 + 1)
                modulate(0, S1, SC1)
                split(1, 1)
                feed_forward(0, G1, G1)
                norm(0, S2)
                finish_vector(SC2)
                dve.wait_ge(x_ready, l * 3 + 2)
                modulate(1, S2, SC2)

                own.did(dve.memset(up[:, :, 0:BUF], 0.0))
                own.did(dve.memset(ul[:, :, 0:CW - 1], 0.0))
                for i in range(IN_UNITS - 1):
                    split(IN + i + 2, (IN + i + 2) % SLOTS)
                    if i < 4:
                        dve.wait_ge(units_done, l * UNITS + (IN + i + 1 + SLOTS))
                        dst, pad = ((up, BUF), (ul, CW - 1))[i // 2]
                        m = 2 * (i % 2)
                        own.did(dve.tensor_copy(dst[:, m, pad:pad + T], bank[2 * (i % 3)][:, 0:T]))
                        dve.tensor_copy(dst[:, m + 1, pad:pad + T], bank[2 * (i % 3) + 1][:, 0:T])\
                           .then_inc(in_read, 1)
                dve.wait_ge(in_read, l * 4 + 4)

                for m in range(WT):
                    own.did(dve.tensor_scalar(xc[:, m, 0:TP], ul[:, m, 0:TP], cwT[:, 0, m:m + 1], cbT[:, m:m + 1],
                                              ALU.mult, ALU.add))
                own.did(dve.tensor_copy(uls[:, :, :, CW - 1], ul[:, :, CW - 1 + TP:]))
                own.wait()
                for k in range(1, CW):
                    for m in range(WT):
                        own.did(dve.scalar_tensor_tensor(xc[:, m, 0:TP], ul[:, m, k:k + TP], cwT[:, k, m:m + 1],
                                                         xc[:, m, 0:TP], ALU.mult, ALU.add))
                    own.wait()
                taps = cwT.rearrange("p k m -> p m k").unsqueeze(2).broadcast_to([P, WT, B, CW])
                own.then(dve.tensor_tensor(prod[:], uls[:], taps, ALU.mult))
                own.then(dve.tensor_reduce(small[:], prod[:], AX_X, ALU.add))
                dve.tensor_tensor(xc[:, :, TP:T], small[:], cbT.unsqueeze(2).broadcast_to([P, WT, B]), ALU.add)\
                   .then_inc(xc_ready, 1)
                split(OUT + 1, (OUT + 1) % SLOTS)
                finish_vector(G2)

                own.then(dve.tensor_tensor(win_a[:, :, 1:TP + BUF], up[:, :, 1:TP + BUF], up[:, :, 0:TP + BUF - 1],
                                           ALU.add))
                for g, (dst, src) in ((1, (win_b, win_a)), (2, (win_a, win_b)), (3, (win_b, win_a))):
                    w = WINDOWS[g]
                    own.then(dve.tensor_tensor(dst[:, g:WT, w - 1:TP + BUF], src[:, g:WT, w - 1:TP + BUF],
                                               src[:, g:WT, w // 2 - 1:TP + BUF - w // 2], ALU.add))
                own.did(dve.tensor_copy(us[:, :, :, BUF], up[:, :, BUF + TP:]))
                for g, w in enumerate(WINDOWS):
                    own.did(dve.scalar_tensor_tensor(z[:, g, 0:TP], (win_a, win_b)[g % 2][:, g, BUF:BUF + TP], 1.0 / w,
                                                     up[:, g, BUF:BUF + TP], ALU.mult, ALU.subtract))
                own.wait()
                for g, w in enumerate(WINDOWS):
                    own.did(dve.tensor_tensor(z[:, g, 0:16], (win_a, win_b)[g % 2][:, g, BUF:BUF + 16],
                                              inv_head[:, g], ALU.mult))
                    own.did(dve.tensor_reduce(small[:, g], us[:, g, :, BUF + 1 - w:BUF + 1], AX_X, ALU.add))
                own.wait()
                own.did(dve.tensor_tensor(z[:, 0:WT, 0:16], z[:, 0:WT, 0:16], up[:, :, BUF:BUF + 16], ALU.subtract))
                for g, w in enumerate(WINDOWS):
                    o = dve.scalar_tensor_tensor(z[:, g, TP:T], small[:, g], 1.0 / w, us[:, g, :, BUF],
                                                 ALU.mult, ALU.subtract)
                    if g < WT - 1:
                        own.did(o)
                o.then_inc(pooled_ready, 1)

                dve.wait_ge(sig_done, (l + 1) * (2 * WT))
                own.then(dve.tensor_tensor(ig[:], ig[:], xc[:], ALU.mult))
                dve.wait_ge(decay_done, (l + 1) * (2 * WT))
                own.then(dve.tensor_scalar(rg[:], tt[:], 1.0, None, ALU.add))
                own.then(dve.reciprocal(rg[:], rg[:]))
                dve.tensor_tensor(tt[:], tt[:], rg[:], ALU.mult).then_inc(ratio_ready, 1)
                finish_vector(G3)
                own.did(dve.tensor_tensor(hs[:, :, TP:T], av[:, :, TP:T], h0[:], ALU.mult))
                dve.wait_ge(root_done, l + 1)
                own.then(dve.tensor_tensor(ig[:], ig[:], rg[:], ALU.mult))
                for m in range(WT):
                    own.did(dve.tensor_tensor_scan(hs[:, m, 0:TP], av[:, m, 0:TP], ig[:, m, 0:TP], 0.0,
                                                   ALU.mult, ALU.add))
                own.then(dve.tensor_tensor(hs[:, :, TP:T], hs[:, :, TP:T], ig[:, :, TP:T], ALU.add))
                dve.wait_ge(gelu_done, l * 2 + 2)
                dve.tensor_tensor(z[:, WT:], z[:, WT:], hs[:], ALU.mult).then_inc(ylru_done, 1)
                for half in range(2):
                    a = half * WT
                    dve.wait_ge(m_hi_done, l * (3 * DT + 2) + (2 * DT + 1 + half))
                    o = dve.tensor_tensor(m_lo[:, a:a + WT], z[:, a:a + WT], m_hi[:, a:a + WT].bitcast(F32),
                                          ALU.subtract)
                    if half:
                        o.then_inc(m_ready, 1)
                    else:
                        own.did(o)
                for i, (m0, n, kh) in enumerate(OUT_PLAN):
                    split(OUT + i + 2, (OUT + i + 2) % SLOTS)
                    if kh:
                        dve.wait_ge(units_done, l * UNITS + (OUT + i + 1 + SLOTS))
                        residual([(m, m % 6) for m in range(m0, m0 + n)], G2, (out_read, l * 3 + (i // 2 + 1)))

                def turn_rows():
                    for i, (b, n) in enumerate(((2, BUF + B), (3, CW - 1 + B), (5, 1 + B))):
                        dve.wait_ge(rows_out, l * 3 + i + 1)
                        dve.tensor_copy(s_rows[32 * i:32 * i + n, :], bank[b][0:n, :]).then_inc(rows_ready, 1)

                norm(1, S3)
                finish_vector(SC3)
                turn_rows()
                dve.wait_ge(x_ready, l * 3 + 3)
                modulate(2, S3, SC3)
                feed_forward(1, G3, None)
                norm(2, None)
                assert own.n == VECTOR_STEPS, own.n

            with dve.Fori(0, DEPTH) as l:
                layer(l)

            y_rows = z[:].rearrange("p m t -> p (m t)")[:, 0:2 * D].rearrange("p (a d) -> p a d", a=2)
            for m in range(DT):
                dve.wait_ge(fin_out, m + 1)
                dve.tensor_copy(y_rows[:, :, m * P:(m + 1) * P], bank[m % 2][:, 0:TP].rearrange("p (a d) -> p a d", a=2))
                dve.tensor_copy(ys_rows[:, m * P:(m + 1) * P], bank[m % 2][0:B, TP:TP + P]).then_inc(fin_read, 1)


_INS = ['x_prompt', 'x_sample', 'state_pool', 'state_conv', 'state_rglru', 'c_prompt', 'c_sample', 'w_ada', 'b_ada',
        'ffn1_wgu', 'ffn1_wdown', 'w_in', 'w_out', 'w_pool', 'pool_scale', 'conv_w', 'conv_b', 'w_rg_a', 'b_rg_a',
        'w_rg_x', 'b_rg_x', 'lru_lambda', 'ffn2_wgu', 'ffn2_wdown', 'ln_g', 'ln_b']


def kernel(**inputs):
    import numpy as _np
    import concourse.bacc as _bacc
    from concourse import mybir as _mybir
    from concourse.bass_utils import run_bass_kernel_spmd as _run

    depth, decs, buf, width = inputs['state_pool'].shape
    cw1 = inputs['state_conv'].shape[2]
    outs = [tuple(inputs['x_prompt'].shape), tuple(inputs['x_sample'].shape), (depth, 1, buf, width),
            (depth, 1, cw1, width), (depth, 1, width), (depth, decs, buf, width), (depth, decs, cw1, width),
            (depth, decs, width)]
    nc = _bacc.Bacc("TRN2", target_bir_lowering=False, num_devices=1)
    arrays, args = {}, []
    for name in _INS:
        a = _np.ascontiguousarray(inputs[name])
        arrays[f"in_{name}_dram"] = a
        args.append(nc.dram_tensor(f"in_{name}_dram", a.shape, _mybir.dt.from_np(a.dtype), kind="ExternalInput").ap())
    for i, shape in enumerate(outs):
        args.append(nc.dram_tensor(f"out_{i}_dram", shape, _mybir.dt.float32, kind="ExternalOutput").ap())
    trunk(nc, *args)
    r = _run(nc, [arrays], core_ids=[0])
    return tuple(r.results[0][f"out_{i}_dram"] for i in range(len(outs)))
```

```python
from contextlib import ExitStack

import concourse.bass as bass
from concourse import mybir
from concourse.alu_op_type import AluOpType as ALU

ACT = mybir.ActivationFunctionType
F32 = mybir.dt.float32
F32R = mybir.dt.float32r
AX_X = mybir.AxisListType.X

P = 128
SLOTS = 3
ADA_SLOTS = 4
WINDOWS = (2, 4, 8, 16)
VECTOR_STEPS = 172


class Own:

    def __init__(self, eng, sem):
        self.eng, self.sem, self.base, self.n = eng, sem, 0, 0

    def did(self, ins):
        ins.then_inc(self.sem, 1)
        self.n += 1

    def wait(self):
        self.eng.wait_ge(self.sem, self.base + self.n)

    def then(self, ins):
        self.did(ins)
        self.wait()


def trunk(nc: bass.Bass, x_prompt, x_sample, state_pool, state_conv, state_rglru, c_prompt, c_sample,
          w_ada, b_ada, ffn1_wgu, ffn1_wdown, w_in, w_out, w_pool, pool_scale, conv_w, conv_b,
          w_rg_a, b_rg_a, w_rg_x, b_rg_x, lru_lambda, ffn2_wgu, ffn2_wdown, ln_g, ln_b,
          y_prompt, y_sample, pool_prompt, conv_prompt, h_prompt, pool_sample, conv_sample, h_sample):
    DEPTH, D, _ = w_in.shape
    TP = x_prompt.shape[1]
    B = x_sample.shape[0]
    T = TP + B
    DT = D // P
    FT = ffn1_wdown.shape[1] // P
    WT = pool_scale.shape[1] // P
    BUF = state_pool.shape[2]
    CW = conv_w.shape[1]
    NMOD = w_ada.shape[2] // D
    HD = w_rg_a.shape[2]
    C = 1 + B
    ALPHA = (2 * DEPTH) ** 0.25
    EPS = 1e-5 / ALPHA ** 2
    LRU_C = 8.0
    assert (TP, DT, FT, WT, CW, HD, BUF) == (256, 8, 21, 4, 4, 64, 15)

    UP_UNITS, DOWN_UNITS, IN_UNITS, OUT_UNITS = FT, 12, 6, 6
    UNITS = 2 * (UP_UNITS + DOWN_UNITS) + IN_UNITS + OUT_UNITS
    UP = (0, UP_UNITS + DOWN_UNITS + IN_UNITS + OUT_UNITS)
    DOWN = (UP[0] + UP_UNITS, UP[1] + UP_UNITS)
    IN = DOWN[0] + DOWN_UNITS
    OUT = IN + IN_UNITS
    ROUNDS = UNITS // SLOTS
    assert UNITS % SLOTS == 0
    OUT_PLAN = [(0, 2, 0), (2, 3, 0), (5, 3, 0), (5, 3, 1), (2, 3, 1), (0, 2, 1)]
    S1, SC1, G1, S2, SC2, G2, S3, SC3, G3 = range(NMOD)
    CHUNKS = 4
    HALVES = 2
    N_PARAM = 17

    with ExitStack() as ctx:
        def sb(name, shape, dt=F32, c=ctx):
            return c.enter_context(nc.sbuf_tensor(name, shape, dt))

        def sem(name):
            return ctx.enter_context(nc.semaphore(name))

        raw = sb("raw", [P, SLOTS, 16 * P])
        w_hi = sb("w_hi", [P, SLOTS, 16 * P], F32R)
        w_lo = sb("w_lo", [P, SLOTS, 16 * P], F32R)
        ada_raw = sb("ada_raw", [P, ADA_SLOTS, DT, 256])
        x = sb("x", [P, DT, T])
        z = sb("z", [P, DT, T])
        m_hi = sb("m_hi", [P, DT, T], F32R)
        m_lo = sb("m_lo", [P, DT, T], F32R)
        with ExitStack() as c1:
            h_hi = sb("h_hi", [P, FT, T], F32R, c1)
            h_lo = sb("h_lo", [P, FT, T], F32R, c1)
        with ExitStack() as c2:
            win_a = sb("win_a", [P, WT, BUF + T], c=c2)
            win_b = sb("win_b", [P, WT, BUF + T], c=c2)
            up = sb("up", [P, WT, BUF + T], c=c2)
            ul = sb("ul", [P, WT, CW - 1 + T], c=c2)
            xc = sb("xc", [P, WT, T], c=c2)
            rg = sb("rg", [P, WT, T], c=c2)
            ig = sb("ig", [P, WT, T], c=c2)
            av = sb("av", [P, WT, T], c=c2)
            tt = sb("tt", [P, WT, T], c=c2)
            hs = sb("hs", [P, WT, T], c=c2)
        with ExitStack() as c3:
            sq = sb("sq", [P, DT, T], c=c3)
        with ExitStack() as c4:
            x_rows = sb("x_rows", [P, TP // P, D], c=c4)
            xs_rows = sb("xs_rows", [B, D], c=c4)
            c_rows = sb("c_rows", [C, D], c=c4)
            ys_rows = sb("ys_rows", [B, D], c=c4)
        sb("region_h", [P, 2 * FT * T])
        gate_act = sb("gate_act", [P, T])
        h_full = sb("h_full", [P, T])
        zsum = sb("zsum", [P, T])
        rstd = sb("rstd", [P, T])
        part = sb("part", [P, HALVES, P])
        coef = sb("coef", [P, 2, DT, C])
        last_ln = sb("last_ln", [P, 2, DT])
        spare = sb("spare", [P, 1])
        mod = sb("mod", [P, NMOD, DT, C])
        cT = sb("cT", [P, DT, 32])
        ident = sb("ident", [P, P])
        mean_w = sb("mean_w", [P, P])
        eps = sb("eps", [P, 1])
        credits = sb("credits", [P, 16])
        inv_head = sb("inv_head", [P, WT, 16])
        p_rows = sb("p_rows", [P, P])
        q_rows = sb("q_rows", [P, P])
        s_rows = sb("s_rows", [P, WT * P])
        r_rows = sb("r_rows", [32, WT * P])
        pT = sb("pT", [P, NMOD * DT + 6 * DT])
        qT = sb("qT", [P, 9 * WT])
        sp = sb("sp", [P, 10, WT])
        us = sb("us", [P, WT, B, BUF + 1])
        uls = sb("uls", [P, WT, B, CW])
        prod = sb("prod", [P, WT, B, CW])
        small = sb("small", [P, WT, B])
        h0 = sb("h0", [P, WT, B])
        wp = sb("wp", [P, WT, P])
        wg = sb("wg", [P, 2, WT, P])
        bank = [ctx.enter_context(nc.psum_tensor(f"bank{i}", [P, 512], F32)) for i in range(8)]
        ADA_PART = (6, 7)
        ADA_OUT = [3] + [6] * (NMOD - 1)
        MEAN, VAR = 4, 5
        GATE_BANKS = (4, 5, 0, 1, 4, 5, 0, 1)

        bias_mod = pT[:, 0:NMOD * DT].rearrange("p (v m) -> p v m", v=NMOD)
        ln_gT = pT[:, NMOD * DT:NMOD * DT + 3 * DT].rearrange("p (v m) -> p v m", v=3)
        ln_bT = pT[:, NMOD * DT + 3 * DT:NMOD * DT + 6 * DT].rearrange("p (v m) -> p v m", v=3)
        pscT, cbT, baT, bxT, lamT = (qT[:, WT * i:WT * (i + 1)] for i in (0, 5, 6, 7, 8))
        cwT = qT[:, WT:5 * WT].rearrange("p (k m) -> p k m", k=CW)
        c8, nc8 = sp[:, 0], sp[:, 1]

        x_landed = sem("x_landed")
        c_landed = sem("c_landed")
        param_landed = sem("param_landed")
        w_landed = [sem(f"w_landed{i}") for i in range(SLOTS)]
        ada_landed = [sem(f"ada_landed{i}") for i in range(ADA_SLOTS)]
        stored = sem("stored")
        y_stored = sem("y_stored")
        consts = sem("consts")
        lo_split = sem("lo_split")
        units_done = sem("units_done")
        gate_read = sem("gate_read")
        up_read = sem("up_read")
        pair_read = sem("pair_read")
        ada_used = sem("ada_used")
        hi_split = sem("hi_split")
        gate_done = sem("gate_done")
        h_hi_done = sem("h_hi_done")
        h_ready = sem("h_ready")
        m_full = sem("m_full")
        m_hi_done = sem("m_hi_done")
        m_ready = sem("m_ready")
        part_ready = sem("part_ready")
        mod_out = sem("mod_out")
        mod_read = sem("mod_read")
        prep_out = sem("prep_out")
        prep_read = sem("prep_read")
        sums_ready = sem("sums_ready")
        stat_out = sem("stat_out")
        centred = sem("centred")
        squared = sem("squared")
        std_ready = sem("std_ready")
        normed = sem("normed")
        x_scaled = sem("x_scaled")
        x_ready = sem("x_ready")
        coef_ready = sem("coef_ready")
        sample_full = sem("sample_full")
        in_read = sem("in_read")
        gates_read = sem("gates_read")
        gelu_done = sem("gelu_done")
        xc_ready = sem("xc_ready")
        gate_mm = sem("gate_mm")
        sig_done = sem("sig_done")
        pooled_ready = sem("pooled_ready")
        pool_mm = sem("pool_mm")
        ypool_done = sem("ypool_done")
        decay_done = sem("decay_done")
        ratio_ready = sem("ratio_ready")
        root_done = sem("root_done")
        ylru_done = sem("ylru_done")
        scan_done = sem("scan_done")
        out_read = sem("out_read")
        rows_out = sem("rows_out")
        rows_ready = sem("rows_ready")
        rows_free = sem("rows_free")
        c_silu = sem("c_silu")
        init_out = sem("init_out")
        init_read = sem("init_read")
        final_x = sem("final_x")
        fin_out = sem("fin_out")
        fin_read = sem("fin_read")
        lam_ready = sem("lam_ready")
        lam_exp = sem("lam_exp")
        vector_steps = sem("vector_steps")

        gu_view = [w.rearrange("l (k p) (h f c) -> l h f p k c", p=P, h=2, c=P) for w in (ffn1_wgu, ffn2_wgu)]
        down_view = [w.rearrange("l (t k p) (m c) -> l t m p k c", t=3, p=P, c=2 * P)
                     for w in (ffn1_wdown, ffn2_wdown)]
        in_view = w_in.rearrange("l (k p) (m c) -> l m p k c", p=P, c=2 * P)
        out_view = w_out.rearrange("l (k p) d -> l p k d", p=P)
        ada_view = w_ada.rearrange("l (k p) (v c d) -> l v c p k d", p=P, v=NMOD, c=CHUNKS)

        block = ctx.enter_context(nc.Block())

        @block.sync
        def _(sync):
            with sync.Fori(0, DEPTH) as l:
                def slot_free(unit):
                    sync.wait_ge(lo_split, l * UNITS + unit + 1)

                def load_unit(unit, slot, halves):
                    slot_free(unit)
                    for dst, src in halves:
                        sync.dma_start(dst, src).then_inc(w_landed[slot], 16)

                def tiles(slot, c):
                    return raw[:, slot].rearrange("p (k c) -> p k c", c=c)

                def load_gate_up(f, tile, unit, slot):
                    half = raw[:, slot].rearrange("p (h k c) -> p h k c", h=2, c=P)
                    load_unit(unit, slot, [(half[:, h], gu_view[f][l, h, tile]) for h in range(2)])

                def load_down(f, pair, third, unit):
                    dst, src = tiles(third, 2 * P), down_view[f][l, third, pair]
                    load_unit(unit, third, [(dst[:, 0:4], src[:, 0:4]), (dst[:, 4:7], src[:, 4:7])])

                def load_ada(v):
                    for c in range(CHUNKS):
                        sync.wait_ge(ada_used, l * (NMOD * CHUNKS) + (v * CHUNKS + c + 1))
                        sync.dma_start(ada_raw[:, c], ada_view[l, v, c]).then_inc(ada_landed[c], 16)

                def load_gate_ups(f, first, end=UP_UNITS // SLOTS):
                    with sync.Fori(first, end) as r:
                        for j in range(SLOTS):
                            load_gate_up(f, r * SLOTS + j, r * SLOTS + (UP[f] + j), j)

                def load_downs(f, first=0, end=DOWN_UNITS // SLOTS):
                    with sync.Fori(first, end) as pair:
                        for third in range(3):
                            load_down(f, pair, third, pair * SLOTS + (DOWN[f] + third))

                load_ada(S1)
                load_gate_up(0, 0, 0, 0)
                load_ada(SC1)
                load_gate_up(0, 1, 1, 1)
                load_gate_up(0, 2, 2, 2)
                load_gate_ups(0, 1, 4)
                load_ada(G1)
                load_gate_ups(0, 4)
                load_downs(0, 0, 2)
                load_ada(S2)
                load_downs(0, 2)
                load_ada(SC2)
                for i in range(IN_UNITS):
                    if i == 3:
                        load_ada(G2)
                    dst = tiles(i % SLOTS, 2 * P)
                    load_unit(IN + i, i % SLOTS, [(dst[:, 4 * k:4 * k + 4], in_view[l, i, :, 4 * k:4 * k + 4])
                                                  for k in range(2)])
                for i, (m, n, kh) in enumerate(OUT_PLAN):
                    if i == 3:
                        load_ada(S3)
                    dst = raw[:, i % SLOTS, 0:4 * n * P].rearrange("p (k c) -> p k c", c=n * P)
                    load_unit(OUT + i, i % SLOTS,
                              [(dst[:, 2 * k:2 * k + 2],
                                out_view[l, :, 4 * kh + 2 * k:4 * kh + 2 * k + 2, m * P:(m + n) * P])
                               for k in range(2)])
                load_ada(SC3)
                for j in range(SLOTS):
                    load_gate_up(1, j, UP[1] + j, j)
                load_ada(G3)
                load_gate_ups(1, 1)
                load_downs(1)

            sync.wait_ge(fin_read, DT)
            y_rows = z[:].rearrange("p m t -> p (m t)")[:, 0:2 * D].rearrange("p (a d) -> p a d", a=2)
            sync.dma_start(y_prompt.rearrange("o (a p) d -> p (o a) d", p=P), y_rows).then_inc(y_stored, 16)
            sync.dma_start(y_sample.rearrange("b o d -> (b o) d"), ys_rows[:]).then_inc(y_stored, 16)
            sync.wait_ge(y_stored, 32)

        @block.gpsimd
        def _(pool):
            pool.memset(ident[:], 0.0).then_inc(consts, 1)
            pool.memset(mean_w[:], 1.0 / D).then_inc(consts, 1)
            pool.memset(cT[:], 0.0).then_inc(consts, 1)
            pool.memset(eps[:], EPS).then_inc(consts, 1)
            pool.memset(wg[:], 0.0).then_inc(consts, 1)
            for g, w in enumerate(WINDOWS):
                pool.memset(inv_head[:, g, w - 1:16], 1.0 / w).then_inc(consts, 1)
                for t in range(w - 1):
                    pool.memset(inv_head[:, g, t:t + 1], 1.0 / (t + 1)).then_inc(consts, 1)
            n = 5 + WT + sum(w - 1 for w in WINDOWS)
            pool.wait_ge(consts, n)
            pool.affine_select(out=ident[:], in_=ident[:], compare_op=ALU.not_equal, fill=1.0, base=0,
                               pattern=[[-1, P]], channel_multiplier=1).then_inc(consts, 1)
            for k, (s, credit) in enumerate(((lo_split, SLOTS), (units_done, SLOTS), (gate_read, 3), (up_read, 3),
                                             (pair_read, 2), (ada_used, ADA_SLOTS), (part_ready, 2),
                                             (mod_read, 1), (h_ready, 1))):
                pool.memset(credits[:, k:k + 1], 0.0).then_inc(s, credit)

            with pool.Fori(0, DEPTH) as l:
                def load(dst, src):
                    pool.dma_start(dst, src).then_inc(param_landed, 16)

                lw = lambda a: a[l].rearrange("(r c) -> r c", c=P)
                nb, nl = NMOD * DT, 3 * DT
                load(p_rows[0:nb, :], lw(b_ada))
                load(p_rows[nb:nb + nl, :], ln_g[l].rearrange("i (r c) -> (i r) c", c=P))
                load(p_rows[nb + nl:nb + 2 * nl, :], ln_b[l].rearrange("i (r c) -> (i r) c", c=P))
                load(q_rows[0:WT, :], lw(pool_scale))
                load(q_rows[WT:5 * WT, :], conv_w[l].rearrange("k (r c) -> (k r) c", c=P))
                for i, a in ((5, conv_b), (6, b_rg_a), (7, b_rg_x), (8, lru_lambda)):
                    load(q_rows[i * WT:(i + 1) * WT, :], lw(a))
                load(s_rows[0:B * BUF, :], state_pool[l].rearrange("b t d -> (b t) d"))
                load(r_rows[0:B * (CW - 1), :], state_conv[l].rearrange("b t d -> (b t) d"))
                load(r_rows[24:24 + B, :], state_rglru[l])
                load(wp[:], w_pool[l].rearrange("g c d -> c g d"))
                for k, a in enumerate((w_rg_a, w_rg_x)):
                    for e in range(2):
                        heads = a[l].rearrange("(m e) i j -> e i m j", e=2)[e]
                        load(wg[HD * e:HD * (e + 1), k, :, HD * e:HD * (e + 1)], heads)
                pool.dma_start(pool_sample[l, :, 0:BUF - 1], state_pool[l, :, 1:BUF]).then_inc(stored, 16)
                pool.dma_start(conv_sample[l, :, 0:CW - 2], state_conv[l, :, 1:CW - 1]).then_inc(stored, 16)
                for i, (g, b) in enumerate(((last_ln[:, 0], last_ln[:, 1]), (ln_gT[:, 0], ln_bT[:, 0]),
                                            (ln_gT[:, 1], ln_bT[:, 1]))):
                    if i == 1:
                        pool.wait_ge(prep_read, l * 2 + 2)
                    wide = lambda a: a[:, m:m + 1].broadcast_to([P, T])
                    for m in range(DT):
                        pool.wait_ge(normed, l * (3 * DT) + (i * DT + m + 1))
                        pool.tensor_tensor(x[:, m], z[:, m], wide(g), ALU.mult).then_inc(x_scaled, 1)
                    for m in range(DT):
                        pool.wait_ge(x_scaled, l * (3 * DT) + (i * DT + m + 1))
                        pool.tensor_tensor(x[:, m], x[:, m], wide(b), ALU.add).then_inc(x_ready, 1)
                pool.wait_ge(rows_ready, (l + 1) * 3)
                for dst, a, b in ((pool_prompt[l, 0], 0, BUF), (pool_sample[l, :, BUF - 1], BUF, BUF + B),
                                  (conv_prompt[l, 0], 32, 32 + CW - 1),
                                  (conv_sample[l, :, CW - 2], 32 + CW - 1, 32 + CW - 1 + B),
                                  (h_prompt[l], 64, 65), (h_sample[l], 65, 65 + B)):
                    pool.dma_start(dst, s_rows[a:b, :]).then_inc(stored, 16)
                pool.wait_ge(stored, (l + 1) * (8 * 16))

        @block.tensor
        def _(pe):
            def transpose_rows(out, rows):
                return pe.transpose(out, rows, ident[0:rows.shape[0], 0:rows.shape[0]])

            pe.wait_ge(consts, 6 + WT + sum(w - 1 for w in WINDOWS))
            pe.wait_ge(c_silu, 1)
            for m in range(DT):
                t = transpose_rows(bank[0][:, m * C:(m + 1) * C], c_rows[:, m * P:(m + 1) * P])
            t.then_inc(init_out, 1)
            pe.wait_ge(x_landed, 32)
            for m in range(DT):
                b = bank[1 + m % 4]
                if m >= 4:
                    pe.wait_ge(normed, m - 3)
                for a in range(TP // P):
                    transpose_rows(b[:, a * P:(a + 1) * P], x_rows[:, a, m * P:(m + 1) * P])
                transpose_rows(b[:, TP:T], xs_rows[:, m * P:(m + 1) * P]).then_inc(init_out, 1)
            pe.wait_ge(init_read, 1)
            pe.wait_ge(normed, DT)

            def layer(l):
                def unit_ready(unit):
                    pe.wait_ge(lo_split, l * UNITS + unit + (1 + SLOTS))

                def product(out, hi, lo, r_hi, r_lo, start, stop, done=None):
                    pe.matmul(out, hi, r_hi, start=start, stop=False)
                    pe.matmul(out, hi, r_lo, start=False, stop=False)
                    mm = pe.matmul(out, lo, r_hi, start=False, stop=stop)
                    if stop and done is not None:
                        mm.then_inc(done, 1)
                    return mm

                def weight(slot, i):
                    return w_hi[:, slot, i * P:(i + 1) * P], w_lo[:, slot, i * P:(i + 1) * P]

                def ada_part(v, h):
                    if h == 0 and v != SC1:
                        pe.wait_ge(mod_read, l * NMOD + (v + 1))
                    for c in (2 * h, 2 * h + 1):
                        pe.wait_ge(ada_landed[c], (l * NMOD + (v + 1)) * 16)
                    pe.wait_ge(part_ready, l * (NMOD * HALVES) + (v * HALVES + h + 1))
                    for k in range(DT):
                        for g in range(4):
                            c, a = 2 * h + g // 2, P * (g % 2)
                            mm = pe.matmul(bank[ADA_PART[h]][32 * g:32 * g + 32, 0:P], cT[:, k, :],
                                           ada_raw[:, c, k, a:a + P], start=k == 0, stop=k == DT - 1,
                                           tile_position=(0, 32 * g))
                            if k == DT - 1 and g % 2:
                                mm.then_inc(ada_used, 1)

                def ada_turn(v, h):
                    pe.wait_ge(part_ready, l * (NMOD * HALVES) + (v * HALVES + h + 3))
                    mm = pe.transpose(bank[ADA_OUT[v]][:, (h + 1) * P:(h + 2) * P], part[:, h], ident[:])
                    if h:
                        mm.then_inc(mod_out, 1)

                def ada_rest(v):
                    ada_part(v, 1)
                    ada_turn(v, 0)
                    ada_turn(v, 1)

                def ada(v):
                    ada_part(v, 0)
                    ada_rest(v)

                def mean(i):
                    pe.wait_ge(sums_ready, l * 3 + (i + 1))
                    pe.matmul(bank[MEAN][:, 0:T], mean_w[:], zsum[:], start=True, stop=True).then_inc(stat_out, 1)

                def variance(i):
                    for m in range(DT):
                        if m % 2 == 0:
                            pe.wait_ge(squared, l * (3 * DT // 2) + (i * DT // 2 + m // 2 + 1))
                        mm = pe.matmul(bank[VAR][:, 0:T], mean_w[:], sq[:, m], start=m == 0, stop=m == DT - 1)
                    mm.then_inc(stat_out, 1)

                def norm_beside(i, v, after):
                    ada_part(v, 0)
                    mean(i)
                    ada_rest(v)
                    variance(i)
                    ada_part(after, 0)

                def inputs_ready(first, k):
                    pe.wait_ge(m_ready, l * (3 * DT + 2) + (first + k + 1))

                def down_pair(f, half, pair):
                    for third in range(3):
                        unit_ready(half * 6 + (DOWN[f] + 3 * pair + third))
                        pe.wait_ge(h_ready, l * (2 * FT) + (f * FT + 7 * (third + 1) + 1))
                        if third == 0:
                            pe.wait_ge(up_read, l * (2 * FT) + (f * FT + FT - 2 + pair + 3))
                            pe.wait_ge(pair_read, l * 8 + half * 2 + (f * 4 + pair + 1))
                        for i in range(2):
                            for k in range(7):
                                mm = product(bank[2 * pair + i][:, 0:T], *weight(third, 2 * k + i),
                                             h_hi[:, 7 * third + k], h_lo[:, 7 * third + k],
                                             third == 0 and k == 0, third == 2 and k == 6)
                        mm.then_inc(units_done, 1)

                def feed_forward(f, vectors):
                    with pe.Fori(0, UP_UNITS // SLOTS) as r:
                        for j in range(SLOTS):
                            if j == 0 and f == 0:
                                pe.wait_ge(prep_read, l * 2 + 2)
                            if j == 1 and f == 1:
                                pe.wait_ge(rows_ready, l * 3 + 3)
                            unit_ready(r * SLOTS + (UP[f] + j))
                            turn = l * (2 * FT) + r * SLOTS + (f * FT + j + 1)
                            pe.wait_ge(gate_read, turn)
                            if j == 0:
                                pe.wait_ge(up_read, turn)
                                for k in range(DT):
                                    inputs_ready(f * (2 * DT + 2), k)
                                    product(bank[2 * j][:, 0:T], *weight(j, k), m_hi[:, k], m_lo[:, k],
                                            k == 0, k == DT - 1, gate_done)
                                    product(bank[2 * j + 1][:, 0:T], *weight(j, DT + k), m_hi[:, k], m_lo[:, k],
                                            k == 0, k == DT - 1, units_done)
                                continue
                            for k in range(DT):
                                product(bank[2 * j][:, 0:T], *weight(j, k), m_hi[:, k], m_lo[:, k],
                                        k == 0, k == DT - 1, gate_done)
                            pe.wait_ge(up_read, turn)
                            for k in range(DT):
                                product(bank[2 * j + 1][:, 0:T], *weight(j, DT + k), m_hi[:, k], m_lo[:, k],
                                        k == 0, k == DT - 1, units_done)
                    if f:
                        ada_rest(vectors[0])
                    else:
                        ada(vectors[0])
                    if len(vectors) > 1:
                        for pair in range(4):
                            down_pair(f, pair // 2, pair % 2)
                            if pair == 1:
                                ada(vectors[1])
                    else:
                        with pe.Fori(0, 2) as half:
                            for pair in range(2):
                                down_pair(f, half, pair)

                ada(S1)
                pe.wait_ge(param_landed, (l + 1) * (16 * N_PARAM))
                for m in range(WT):
                    transpose_rows(bank[0][:, m * 120:(m + 1) * 120], s_rows[0:B * BUF, m * P:(m + 1) * P])
                for m in range(WT):
                    transpose_rows(bank[1][:, m * 32:(m + 1) * 32], r_rows[:, m * P:(m + 1) * P])
                transpose_rows(bank[1][:, 128:248], p_rows[0:120, :])
                transpose_rows(bank[1][:, 248:284], q_rows[0:36, :]).then_inc(prep_out, 1)

                ada(SC1)
                feed_forward(0, [G1, S2])
                norm_beside(0, SC2, G2)

                def recurrence_gates():
                    pe.wait_ge(xc_ready, l + 1)
                    pe.wait_ge(in_read, l * 4 + 4)
                    for i, b in enumerate(GATE_BANKS):
                        if i >= 4:
                            pe.wait_ge(sig_done, l * (2 * WT) + i - 3)
                        pe.matmul(bank[b][:, 0:T], wg[:, i // WT, i % WT, :], xc[:, i % WT, :],
                                  start=True, stop=True).then_inc(gate_mm, 1)

                for u in range(IN_UNITS):
                    if u == 4:
                        ada_rest(G2)
                    if u == 5:
                        recurrence_gates()
                        pe.wait_ge(sig_done, l * (2 * WT) + 6)
                    unit_ready(IN + u)
                    if u == 3:
                        pe.wait_ge(in_read, l * 4 + 1)
                    steps = [(i, k) for i in range(2) for k in range(DT)]
                    if u == 0:
                        steps.sort(key=lambda step: step[1])
                    for i, k in steps:
                        if u == 0 and i == 0:
                            inputs_ready(DT, k)
                        mm = product(bank[2 * (u % 3) + i][:, 0:T], *weight(u % SLOTS, 2 * k + i),
                                     m_hi[:, k], m_lo[:, k], k == 0, k == DT - 1)
                    mm.then_inc(units_done, 1)
                pe.wait_ge(pooled_ready, l + 1)
                pe.wait_ge(sig_done, (l + 1) * (2 * WT))
                for g in range(WT):
                    if g == 2:
                        pe.wait_ge(gates_read, l * 2 + 1)
                    pe.matmul(bank[g][:, 0:T], wp[:, g, :], z[:, g, :], start=True, stop=True)\
                      .then_inc(pool_mm, 1)
                ada(S3)

                pe.wait_ge(ypool_done, l * WT + WT)
                pe.wait_ge(gates_read, l * 2 + 2)
                pe.wait_ge(mod_read, l * NMOD + (S3 + 2))
                for i, (m0, n, kh) in enumerate(OUT_PLAN):
                    unit_ready(OUT + i)
                    if i % 3 == 0:
                        inputs_ready(2 * DT, kh)
                    for m in range(n):
                        for k in range(4):
                            mm = product(bank[m0 + m][:, 0:T], *weight(i % SLOTS, k * n + m),
                                         m_hi[:, 4 * kh + k], m_lo[:, 4 * kh + k],
                                         kh == 0 and k == 0, kh == 1 and k == 3)
                    mm.then_inc(units_done, 1)

                def turn_rows():
                    for b, src, a, n in ((2, up, TP, BUF + B), (3, ul, TP, CW - 1 + B), (4, hs, TP - 1, 1 + B)):
                        for m in range(WT):
                            t = pe.transpose(bank[b][0:n, m * P:(m + 1) * P], src[:, m, a:a + n], ident[:])
                        t.then_inc(rows_out, 1)

                pe.wait_ge(out_read, l * 3 + 1)
                norm_beside(1, SC3, G3)
                turn_rows()
                feed_forward(1, [G3])
                mean(2)
                variance(2)

            with pe.Fori(0, DEPTH) as l:
                layer(l)

            for m in range(DT):
                pe.wait_ge(final_x, m + 1)
                b = bank[m % 2]
                if m >= 2:
                    pe.wait_ge(fin_read, m - 1)
                for a in range(TP // P):
                    pe.transpose(b[:, a * P:(a + 1) * P], x[:, m, a * P:(a + 1) * P], ident[:])
                pe.transpose(b[0:B, TP:TP + P], x[:, m, TP:T], ident[:]).then_inc(fin_out, 1)

        @block.scalar
        def _(act):
            act.dma_start(c_rows[0:1, :], c_prompt).then_inc(c_landed, 16)
            act.dma_start(c_rows[1:C, :], c_sample).then_inc(c_landed, 16)
            act.dma_start(xs_rows[:], x_sample.rearrange("b o d -> (b o) d")).then_inc(x_landed, 16)
            act.dma_start(x_rows[:], x_prompt.rearrange("o (a p) d -> p (o a) d", p=P)).then_inc(x_landed, 16)
            act.wait_ge(c_landed, 32)
            act.activation(c_rows[:], c_rows[:], ACT.Silu).then_inc(c_silu, 1)

            def layer(l):
                def split(unit, rounds, slot):
                    act.wait_ge(w_landed[slot], (l * ROUNDS + rounds + 1) * 32)
                    act.wait_ge(units_done, l * UNITS + unit + 1)
                    act.activation(w_hi[:, slot], raw[:, slot], ACT.Copy).then_inc(hi_split, 1)

                def split_at(unit):
                    split(unit, unit // SLOTS, unit % SLOTS)

                def ada_copy(v, halves=(0, 1)):
                    for h in halves:
                        act.wait_ge(ada_used, l * (NMOD * CHUNKS) + (v * CHUNKS + 2 * h + 2 + ADA_SLOTS))
                        act.activation(part[:, h], bank[ADA_PART[h]][:, 0:P], ACT.Copy).then_inc(part_ready, 1)

                def norm(i, v):
                    act.activation(spare[:], eps[:], ACT.Sqrt)
                    if v is not None:
                        ada_copy(v, (0,))
                    for g in range(DT // 2):
                        act.wait_ge(centred, l * (3 * DT // 2) + (i * DT // 2 + g + 1))
                        act.activation(sq[:, 2 * g:2 * g + 2], z[:, 2 * g:2 * g + 2], ACT.Square).then_inc(squared, 1)
                    if v is not None:
                        ada_copy(v, (1,))
                    act.wait_ge(stat_out, l * 6 + (2 * i + 2))
                    act.activation(rstd[:], bank[VAR][:, 0:T], ACT.Sqrt, bias=eps[:]).then_inc(std_ready, 1)

                def modulate(i):
                    first = (0, DT, 2 * DT + 2)[i]
                    act.wait_ge(coef_ready, l * 3 + (i + 1))
                    for m in range(DT + 1):
                        if m < DT:
                            act.wait_ge(normed, l * (3 * DT) + (i * DT + m + 1))
                            act.activation(sq[:, m, 0:TP], z[:, m, 0:TP], ACT.Identity, scale=coef[:, 0, m, 0:1],
                                           bias=coef[:, 1, m, 0:1]).then_inc(m_full, 1)
                        if m == 0:
                            act.wait_ge(sample_full, l * 3 + (i + 1))
                        else:
                            act.wait_ge(m_full, l * (3 * DT) + (i * DT + m))
                            act.activation(m_hi[:, m - 1], sq[:, m - 1], ACT.Copy).then_inc(m_hi_done, 1)

                def feed_forward(f, vectors):
                    with act.Fori(0, UP_UNITS // SLOTS) as r:
                        for j in range(SLOTS):
                            n = UP[f] + j + 2
                            split(r * SLOTS + n, r + n // SLOTS, n % SLOTS)
                            turn = l * (2 * FT) + r * SLOTS + (f * FT + j + 1)
                            act.wait_ge(gate_done, turn)
                            act.activation(gate_act[:], bank[2 * j][:, 0:T], ACT.Silu).then_inc(gate_read, 1)
                            act.wait_ge(up_read, turn + 3)
                            act.activation(h_hi[:, r * SLOTS + j], h_full[:], ACT.Copy).then_inc(h_hi_done, 1)
                    ada_copy(vectors[0])
                    for i in range(DOWN_UNITS - (2 if f else 0)):
                        split_at(DOWN[f] + i + 2)
                        if i == 1 and f == 0:
                            act.wait_ge(lam_ready, l + 1)
                            act.activation(sp[:, 4], sp[:, 3], ACT.Exp).then_inc(lam_exp, 1)
                        if i == 5 and len(vectors) > 1:
                            ada_copy(vectors[1])

                split_at(0)
                ada_copy(S1)
                ada_copy(SC1)
                modulate(0)
                split_at(1)
                feed_forward(0, [G1, S2])
                norm(0, SC2)
                modulate(1)
                for i in range(IN_UNITS):
                    if i == 4:
                        ada_copy(G2)
                    split_at(IN + i + 2)
                    if i == 5:
                        act.wait_ge(ratio_ready, l + 1)
                        act.activation(rg[:], tt[:], ACT.Sqrt).then_inc(root_done, 1)
                    if i >= 4:
                        act.wait_ge(x_ready, l * (3 * DT) + 2 * DT)
                        act.wait_ge(units_done, l * UNITS + IN + i + 1 + SLOTS)
                        for j in range(2):
                            o = act.activation(z[:, WT + 2 * (i - 4) + j], bank[2 * (i % 3) + j][:, 0:T],
                                               ACT.Copy)
                        o.then_inc(gates_read, 1)
                    if i == 4:
                        for n, gb in enumerate(GATE_BANKS):
                            act.wait_ge(gate_mm, l * (2 * WT) + n + 1)
                            dst, b = ((rg, baT), (ig, bxT))[n // WT]
                            m = n % WT
                            act.activation(dst[:, m], bank[gb][:, 0:T], ACT.Sigmoid,
                                           bias=b[:, m:m + 1]).then_inc(sig_done, 1)
                        act.wait_ge(sig_done, (l + 1) * (2 * WT))
                        for m in range(WT):
                            act.activation(tt[:, m], rg[:, m], ACT.Tanh, scale=c8[:, m:m + 1])\
                               .then_inc(decay_done, 1)
                        for m in range(WT):
                            act.activation(av[:, m], rg[:, m], ACT.Exp, scale=nc8[:, m:m + 1])\
                               .then_inc(decay_done, 1)
                for g in range(WT):
                    act.wait_ge(pool_mm, l * WT + g + 1)
                    act.activation(z[:, g], bank[g][:, 0:T], ACT.Copy, scale=pscT[:, g:g + 1])\
                       .then_inc(ypool_done, 1)
                act.wait_ge(ypool_done, (l + 1) * WT)
                act.activation(m_hi[:, 0:WT], z[:, 0:WT], ACT.Copy).then_inc(m_hi_done, 1)
                act.wait_ge(gates_read, l * 2 + 2)
                act.activation(z[:, WT:], z[:, WT:], ACT.Gelu_apprx_tanh).then_inc(gelu_done, 1)
                ada_copy(S3, (0,))
                act.wait_ge(ylru_done, l + 1)
                act.activation(m_hi[:, WT:], z[:, WT:], ACT.Copy).then_inc(m_hi_done, 1)
                ada_copy(S3, (1,))
                for i in range(OUT_UNITS):
                    split_at(OUT + i + 2)
                norm(1, SC3)
                modulate(2)
                feed_forward(1, [G3])
                norm(2, None)

            with act.Fori(0, DEPTH) as l:
                layer(l)

        @block.vector
        def _(dve):
            own = Own(dve, vector_steps)
            n_consts = 6 + WT + sum(w - 1 for w in WINDOWS)
            dve.wait_ge(consts, n_consts)
            own.did(dve.memset(last_ln[:, 0], 1.0))
            own.did(dve.memset(last_ln[:, 1], 0.0))
            dve.wait_ge(init_out, 1)
            dve.tensor_copy(cT[:, :, 0:C], bank[0][:, 0:DT * C].rearrange("p (m c) -> p m c", c=C))\
               .then_inc(init_read, 1)
            for m in range(DT):
                dve.wait_ge(init_out, 2 + m)
                dve.tensor_copy(z[:, m], bank[1 + m % 4][:, 0:T]).then_inc(normed, 1)
            prologue = own.n

            def layer(l):
                own.base, own.n = l * VECTOR_STEPS + prologue, 0

                def split(unit, slot):
                    dve.wait_ge(hi_split, l * UNITS + unit + 1)
                    dve.tensor_tensor(w_lo[:, slot], raw[:, slot], w_hi[:, slot].bitcast(F32), ALU.subtract)\
                       .then_inc(lo_split, 1)

                def finish_vector(v):
                    dve.wait_ge(mod_out, l * NMOD + (v + 1))
                    turned = bank[ADA_OUT[v]][:, P:3 * P].rearrange("p (m c) -> p m c", c=32)[:, :, 0:C]
                    dve.tensor_tensor(mod[:, v], turned, bias_mod[:, v].unsqueeze(2).broadcast_to([P, DT, C]), ALU.add)\
                       .then_inc(mod_read, 1)
                    if v in (G1, G2, G3):
                        factor = (1.0 if v == G2 else 0.5) / ALPHA
                        dve.wait_ge(mod_read, l * NMOD + (v + 2))
                        own.did(dve.tensor_scalar(mod[:, v], mod[:, v], factor, factor, ALU.mult, ALU.add))

                def coefficients(shift, scale, g, b):
                    own.wait()
                    dve.wait_ge(mod_read, l * NMOD + (scale + 2))
                    g, b = (a.unsqueeze(2).broadcast_to([P, DT, C]) for a in (g, b))
                    own.then(dve.tensor_tensor(coef[:, 1], mod[:, scale], b, ALU.mult))
                    own.did(dve.tensor_tensor(coef[:, 1], coef[:, 1], mod[:, shift], ALU.add))
                    dve.tensor_tensor(coef[:, 0], mod[:, scale], g, ALU.mult).then_inc(coef_ready, 1)

                def modulate_samples(i):
                    dve.wait_ge(coef_ready, l * 3 + (i + 1))
                    own.then(dve.tensor_tensor(sq[:, :, TP:T], z[:, :, TP:T], coef[:, 0, :, 1:C], ALU.mult))
                    dve.tensor_tensor(sq[:, :, TP:T], sq[:, :, TP:T], coef[:, 1, :, 1:C], ALU.add)\
                       .then_inc(sample_full, 1)

                def split_input(i):
                    for m in range(DT):
                        dve.wait_ge(m_hi_done, l * (3 * DT + 2) + (m + 1 + (0, DT, 2 * DT + 2)[i]))
                        dve.tensor_tensor(m_lo[:, m], sq[:, m], m_hi[:, m].bitcast(F32), ALU.subtract)\
                           .then_inc(m_ready, 1)

                def residual(tiles, gate, read, first, last):
                    own.wait()
                    for m, b in tiles:
                        dve.wait_ge(x_ready, l * (3 * DT) + ({G1: 0, G2: DT, G3: 2 * DT}[gate] + m + 1))
                        own.did(dve.scalar_tensor_tensor(z[:, m, 0:TP], bank[b][:, 0:TP], mod[:, gate, m, 0:1],
                                                         x[:, m, 0:TP], ALU.mult, ALU.add))
                        o = dve.tensor_tensor(z[:, m, TP:T], bank[b][:, TP:T], mod[:, gate, m, 1:C], ALU.mult)
                        if (m, b) != tiles[-1]:
                            own.did(o)
                    o.then_inc(read[0], 1)
                    dve.wait_ge(*read)
                    m0, n = tiles[0][0], len(tiles)
                    own.then(dve.tensor_tensor(z[:, m0:m0 + n, TP:T], z[:, m0:m0 + n, TP:T],
                                               x[:, m0:m0 + n, TP:T], ALU.add))
                    for m, _ in tiles:
                        if m == first:
                            own.then(dve.tensor_copy(zsum[:], z[:, m]))
                        elif m != last:
                            own.then(dve.tensor_tensor(zsum[:], zsum[:], z[:, m], ALU.add))
                        else:
                            dve.tensor_tensor(zsum[:], zsum[:], z[:, m], ALU.add).then_inc(sums_ready, 1)

                def norm(i, shift=None, scale=None, unit=None):
                    dve.wait_ge(stat_out, l * 6 + (2 * i + 1))
                    for g in range(DT // 2):
                        a = 2 * g
                        dve.tensor_tensor(z[:, a:a + 2], z[:, a:a + 2],
                                          bank[MEAN][:, 0:T].unsqueeze(1).broadcast_to([P, 2, T]),
                                          ALU.subtract).then_inc(centred, 1)
                    if unit is not None:
                        split(unit, unit % SLOTS)
                    if scale is not None:
                        finish_vector(scale)
                        coefficients(shift, scale, ln_gT[:, i], ln_bT[:, i])
                    dve.wait_ge(centred, (l * 3 + (i + 1)) * (DT // 2))
                    dve.wait_ge(std_ready, l * 3 + (i + 1))
                    own.did(dve.reciprocal(rstd[:], rstd[:]))
                    own.wait()
                    own.then(dve.tensor_tensor(z[:, :, TP:T], z[:, :, TP:T],
                                               rstd[:, TP:T].unsqueeze(1).broadcast_to([P, DT, B]), ALU.mult))
                    for m in range(DT):
                        dve.tensor_tensor(z[:, m, 0:TP], z[:, m, 0:TP], rstd[:, 0:TP], ALU.mult).then_inc(normed, 1)
                        if m == 1 and scale is not None:
                            modulate_samples(i + 1)

                def negative_lambda():
                    own.did(dve.tensor_scalar(sp[:, 2], lamT, -1.0, None, ALU.mult))
                    own.wait()
                    dve.tensor_tensor(sp[:, 3], sp[:, 2], lamT, ALU.min).then_inc(lam_ready, 1)
                    dve.wait_ge(lam_ready, l + 1)

                def softplus():
                    own.did(dve.tensor_scalar(sp[:, 2], sp[:, 2], 0.0, None, ALU.max))
                    dve.wait_ge(lam_exp, l + 1)
                    e, zz, z2, p = sp[:, 4], sp[:, 5], sp[:, 6], sp[:, 7]
                    own.then(dve.tensor_scalar(zz, e, 2.0, None, ALU.add))
                    own.then(dve.reciprocal(zz, zz))
                    own.then(dve.tensor_tensor(zz, zz, e, ALU.mult))
                    own.then(dve.tensor_tensor(z2, zz, zz, ALU.mult))
                    own.then(dve.tensor_scalar(p, z2, 1.0 / 17, None, ALU.mult))
                    for d in (15, 13, 11, 9, 7, 5, 3):
                        own.then(dve.scalar_tensor_tensor(p, p, 1.0 / d, z2, ALU.add, ALU.mult))
                    own.then(dve.scalar_tensor_tensor(p, p, 1.0, zz, ALU.add, ALU.mult))
                    own.then(dve.scalar_tensor_tensor(p, p, 2.0, sp[:, 2], ALU.mult, ALU.add))
                    own.did(dve.tensor_scalar(c8, p, LRU_C, None, ALU.mult))
                    own.did(dve.tensor_scalar(nc8, p, -LRU_C, None, ALU.mult))

                def feed_forward(f, gate, between):
                    with dve.Fori(0, UP_UNITS // SLOTS) as r:
                        for j in range(SLOTS):
                            n = UP[f] + j + 2
                            split(r * SLOTS + n, n % SLOTS)
                            turn = l * (2 * FT) + r * SLOTS + (f * FT + j + 1)
                            dve.wait_ge(units_done, l * UNITS + r * SLOTS + (UP[f] + j + 1 + SLOTS))
                            dve.wait_ge(gate_read, turn + 3)
                            dve.wait_ge(h_ready, turn)
                            dve.tensor_tensor(h_full[:], gate_act[:], bank[2 * j + 1][:, 0:T], ALU.mult)\
                               .then_inc(up_read, 1)
                            dve.wait_ge(h_hi_done, turn)
                            dve.tensor_tensor(h_lo[:, r * SLOTS + j], h_full[:],
                                              h_hi[:, r * SLOTS + j].bitcast(F32), ALU.subtract)\
                               .then_inc(h_ready, 1)
                    finish_vector(between[0])
                    for i in range(DOWN_UNITS):
                        n = DOWN[f] + i + 2
                        if n < UNITS and i < DOWN_UNITS - 1:
                            split(n, n % SLOTS)
                        if i == 0 and f == 0:
                            negative_lambda()
                        if i == 3 and f == 0:
                            softplus()
                        if i == 5 and len(between) > 1:
                            finish_vector(between[1])
                        if i % 3 == 2:
                            pair = i // 3
                            dve.wait_ge(units_done, l * UNITS + (DOWN[f] + i + 1 + SLOTS))
                            residual([(2 * pair + i, 2 * (pair % 2) + i) for i in range(2)], gate,
                                     (pair_read, l * 8 + (f * 4 + pair + 1 + 2)), 0, DT - 1)

                split(0, 0)
                dve.wait_ge(prep_out, l + 1)
                own.did(dve.tensor_copy(pT[:], bank[1][:, 128:248]))
                own.wait()
                scales = bias_mod[:, SC1::SC2 - SC1]
                own.did(dve.tensor_scalar(scales, scales, 1.0, None, ALU.add))
                own.did(dve.tensor_copy(qT[:], bank[1][:, 248:284]))
                turned = bank[1][:, 0:WT * 32].rearrange("p (m r) -> p m r", r=32)
                for m in range(WT):
                    own.did(dve.tensor_copy(uls[:, m, :, 0:CW - 1],
                                            turned[:, m, 0:B * (CW - 1)].rearrange("p (b t) -> p b t", b=B)))
                dve.tensor_copy(h0[:], turned[:, :, 24:24 + B]).then_inc(prep_read, 1)
                for m in range(WT):
                    o = dve.tensor_copy(us[:, m, :, 0:BUF],
                                        bank[0][:, m * B * BUF:(m + 1) * B * BUF].rearrange("p (b t) -> p b t", b=B))
                    if m < WT - 1:
                        own.did(o)
                    else:
                        o.then_inc(prep_read, 1)
                dve.wait_ge(prep_read, (l + 1) * 2)
                finish_vector(S1)
                finish_vector(SC1)
                coefficients(S1, SC1, last_ln[:, 0], last_ln[:, 1])
                modulate_samples(0)
                split_input(0)
                dve.wait_ge(x_ready, l * (3 * DT) + DT)
                own.did(dve.tensor_copy(last_ln[:, 0], ln_gT[:, 2]))
                own.did(dve.tensor_copy(last_ln[:, 1], ln_bT[:, 2]))
                split(1, 1)
                feed_forward(0, G1, [G1, S2])
                norm(0, S2, SC2, IN + 1)
                split_input(1)

                own.did(dve.memset(up[:, :, 0:BUF], 0.0))
                own.did(dve.memset(ul[:, :, 0:CW - 1], 0.0))
                def convolve():
                    for m in range(WT):
                        own.did(dve.tensor_scalar(xc[:, m, 0:TP], ul[:, m, 0:TP], cwT[:, 0, m:m + 1], cbT[:, m:m + 1],
                                                  ALU.mult, ALU.add))
                    own.did(dve.tensor_copy(uls[:, :, :, CW - 1], ul[:, :, CW - 1 + TP:]))
                    own.wait()
                    for k in range(1, CW):
                        for m in range(WT):
                            own.did(dve.scalar_tensor_tensor(xc[:, m, 0:TP], ul[:, m, k:k + TP], cwT[:, k, m:m + 1],
                                                             xc[:, m, 0:TP], ALU.mult, ALU.add))
                        own.wait()
                    taps = cwT.rearrange("p k m -> p m k").unsqueeze(2).broadcast_to([P, WT, B, CW])
                    own.then(dve.tensor_tensor(prod[:], uls[:], taps, ALU.mult))
                    own.then(dve.tensor_reduce(small[:], prod[:], AX_X, ALU.add))
                    dve.tensor_tensor(xc[:, :, TP:T], small[:], cbT.unsqueeze(2).broadcast_to([P, WT, B]), ALU.add)\
                       .then_inc(xc_ready, 1)

                def windows():
                    dve.wait_ge(x_ready, l * (3 * DT) + 2 * DT)

                    own.then(dve.tensor_tensor(win_a[:, :, 1:TP + BUF], up[:, :, 1:TP + BUF], up[:, :, 0:TP + BUF - 1],
                                               ALU.add))
                    for g, (dst, src) in ((1, (win_b, win_a)), (2, (win_a, win_b)), (3, (win_b, win_a))):
                        w = WINDOWS[g]
                        own.then(dve.tensor_tensor(dst[:, g:WT, w - 1:TP + BUF], src[:, g:WT, w - 1:TP + BUF],
                                                   src[:, g:WT, w // 2 - 1:TP + BUF - w // 2], ALU.add))
                    own.did(dve.tensor_copy(us[:, :, :, BUF], up[:, :, BUF + TP:]))
                    for g, w in enumerate(WINDOWS):
                        own.did(dve.scalar_tensor_tensor(z[:, g, 0:TP], (win_a, win_b)[g % 2][:, g, BUF:BUF + TP], 1.0 / w,
                                                         up[:, g, BUF:BUF + TP], ALU.mult, ALU.subtract))
                    own.wait()
                    for g, w in enumerate(WINDOWS):
                        own.did(dve.tensor_tensor(z[:, g, 0:16], (win_a, win_b)[g % 2][:, g, BUF:BUF + 16],
                                                  inv_head[:, g], ALU.mult))
                        own.did(dve.tensor_reduce(small[:, g], us[:, g, :, BUF + 1 - w:BUF + 1], AX_X, ALU.add))
                    own.wait()
                    own.did(dve.tensor_tensor(z[:, 0:WT, 0:16], z[:, 0:WT, 0:16], up[:, :, BUF:BUF + 16], ALU.subtract))
                    for g, w in enumerate(WINDOWS):
                        o = dve.scalar_tensor_tensor(z[:, g, TP:T], small[:, g], 1.0 / w, us[:, g, :, BUF],
                                                     ALU.mult, ALU.subtract)
                        if g < WT - 1:
                            own.did(o)
                    o.then_inc(pooled_ready, 1)

                for i in range(4):
                    split(IN + i + 2, (IN + i + 2) % SLOTS)
                    dve.wait_ge(units_done, l * UNITS + (IN + i + 1 + SLOTS))
                    dst, pad = ((up, BUF), (ul, CW - 1))[i // 2]
                    m = 2 * (i % 2)
                    own.did(dve.tensor_copy(dst[:, m, pad:pad + T], bank[2 * (i % 3)][:, 0:T]))
                    dve.tensor_copy(dst[:, m + 1, pad:pad + T], bank[2 * (i % 3) + 1][:, 0:T])\
                       .then_inc(in_read, 1)
                dve.wait_ge(in_read, l * 4 + 4)
                convolve()
                finish_vector(G2)
                split(OUT, OUT % SLOTS)
                windows()

                dve.wait_ge(sig_done, (l + 1) * (2 * WT))
                own.did(dve.tensor_tensor(ig[:], ig[:], xc[:], ALU.mult))
                dve.wait_ge(decay_done, (l + 1) * (2 * WT))
                own.then(dve.tensor_tensor(rg[:], av[:], av[:], ALU.mult))
                dve.scalar_tensor_tensor(tt[:], rg[:], 1.0, tt[:], ALU.add, ALU.mult).then_inc(ratio_ready, 1)
                own.did(dve.tensor_tensor(hs[:, :, TP:T], av[:, :, TP:T], h0[:], ALU.mult))
                split(OUT + 1, (OUT + 1) % SLOTS)
                dve.wait_ge(root_done, l + 1)
                own.then(dve.tensor_tensor(ig[:], ig[:], rg[:], ALU.mult))
                for m in range(WT):
                    own.did(dve.tensor_tensor_scan(hs[:, m, 0:TP], av[:, m, 0:TP], ig[:, m, 0:TP], 0.0,
                                                   ALU.mult, ALU.add))
                own.then(dve.tensor_tensor(hs[:, :, TP:T], hs[:, :, TP:T], ig[:, :, TP:T], ALU.add))
                own.wait()
                dve.wait_ge(m_hi_done, l * (3 * DT + 2) + (2 * DT + 1))
                dve.tensor_tensor(m_lo[:, 0:WT], z[:, 0:WT], m_hi[:, 0:WT].bitcast(F32), ALU.subtract)\
                   .then_inc(m_ready, 1)
                dve.wait_ge(gelu_done, l + 1)
                dve.tensor_tensor(z[:, WT:], z[:, WT:], hs[:], ALU.mult).then_inc(ylru_done, 1)
                dve.wait_ge(m_hi_done, l * (3 * DT + 2) + (2 * DT + 2))
                dve.tensor_tensor(m_lo[:, WT:], z[:, WT:], m_hi[:, WT:].bitcast(F32), ALU.subtract)\
                   .then_inc(m_ready, 1)
                finish_vector(S3)
                for i, (m0, n, kh) in enumerate(OUT_PLAN):
                    if kh:
                        dve.wait_ge(units_done, l * UNITS + (OUT + i + 1 + SLOTS))
                        residual([(m, m) for m in range(m0, m0 + n)], G2, (out_read, l * 3 + (i - 2)), 5, 1)
                    if i < OUT_UNITS - 1:
                        split(OUT + i + 2, (OUT + i + 2) % SLOTS)

                def turn_rows():
                    for i, (b, n) in enumerate(((2, BUF + B), (3, CW - 1 + B), (4, 1 + B))):
                        dve.wait_ge(rows_out, l * 3 + i + 1)
                        dve.tensor_copy(s_rows[32 * i:32 * i + n, :], bank[b][0:n, :]).then_inc(rows_ready, 1)

                norm(1, S3, SC3, UP[1] + 1)
                split_input(2)
                turn_rows()
                feed_forward(1, G3, [G3])
                norm(2)
                assert own.n == VECTOR_STEPS, own.n

            with dve.Fori(0, DEPTH) as l:
                layer(l)

            for m in range(DT):
                dve.wait_ge(normed, DEPTH * (3 * DT) + m + 1)
                dve.tensor_scalar(x[:, m], z[:, m], ln_gT[:, 2, m:m + 1], ln_bT[:, 2, m:m + 1], ALU.mult, ALU.add)\
                   .then_inc(final_x, 1)
            y_rows = z[:].rearrange("p m t -> p (m t)")[:, 0:2 * D].rearrange("p (a d) -> p a d", a=2)
            dve.wait_ge(final_x, DT)
            for m in range(DT):
                dve.wait_ge(fin_out, m + 1)
                dve.tensor_copy(y_rows[:, :, m * P:(m + 1) * P], bank[m % 2][:, 0:TP].rearrange("p (a d) -> p a d", a=2))
                dve.tensor_copy(ys_rows[:, m * P:(m + 1) * P], bank[m % 2][0:B, TP:TP + P]).then_inc(fin_read, 1)


_INS = ['x_prompt', 'x_sample', 'state_pool', 'state_conv', 'state_rglru', 'c_prompt', 'c_sample', 'w_ada', 'b_ada',
        'ffn1_wgu', 'ffn1_wdown', 'w_in', 'w_out', 'w_pool', 'pool_scale', 'conv_w', 'conv_b', 'w_rg_a', 'b_rg_a',
        'w_rg_x', 'b_rg_x', 'lru_lambda', 'ffn2_wgu', 'ffn2_wdown', 'ln_g', 'ln_b']


def kernel(**inputs):
    import numpy as _np
    import concourse.bacc as _bacc
    from concourse import mybir as _mybir
    from concourse.bass_utils import run_bass_kernel_spmd as _run

    depth, decs, buf, width = inputs['state_pool'].shape
    cw1 = inputs['state_conv'].shape[2]
    outs = [tuple(inputs['x_prompt'].shape), tuple(inputs['x_sample'].shape), (depth, 1, buf, width),
            (depth, 1, cw1, width), (depth, 1, width), (depth, decs, buf, width), (depth, decs, cw1, width),
            (depth, decs, width)]
    nc = _bacc.Bacc("TRN2", target_bir_lowering=False, num_devices=1)
    arrays, args = {}, []
    for name in _INS:
        a = _np.ascontiguousarray(inputs[name])
        arrays[f"in_{name}_dram"] = a
        args.append(nc.dram_tensor(f"in_{name}_dram", a.shape, _mybir.dt.from_np(a.dtype), kind="ExternalInput").ap())
    for i, shape in enumerate(outs):
        args.append(nc.dram_tensor(f"out_{i}_dram", shape, _mybir.dt.float32, kind="ExternalOutput").ap())
    trunk(nc, *args)
    r = _run(nc, [arrays], core_ids=[0])
    return tuple(r.results[0][f"out_{i}_dram"] for i in range(len(outs)))
```

```python
from contextlib import ExitStack

import concourse.bass as bass
from concourse import mybir
from concourse.alu_op_type import AluOpType as ALU

ACT = mybir.ActivationFunctionType
F32 = mybir.dt.float32
F32R = mybir.dt.float32r
AX_X = mybir.AxisListType.X

P = 128
SLOTS = 3
ADA_SLOTS = 4
WINDOWS = (2, 4, 8, 16)
VECTOR_STEPS = 173


class Own:

    def __init__(self, eng, sem):
        self.eng, self.sem, self.base, self.n = eng, sem, 0, 0

    def did(self, ins):
        ins.then_inc(self.sem, 1)
        self.n += 1

    def wait(self):
        self.eng.wait_ge(self.sem, self.base + self.n)

    def then(self, ins):
        self.did(ins)
        self.wait()


def trunk(nc: bass.Bass, x_prompt, x_sample, state_pool, state_conv, state_rglru, c_prompt, c_sample,
          w_ada, b_ada, ffn1_wgu, ffn1_wdown, w_in, w_out, w_pool, pool_scale, conv_w, conv_b,
          w_rg_a, b_rg_a, w_rg_x, b_rg_x, lru_lambda, ffn2_wgu, ffn2_wdown, ln_g, ln_b,
          y_prompt, y_sample, pool_prompt, conv_prompt, h_prompt, pool_sample, conv_sample, h_sample):
    DEPTH, D, _ = w_in.shape
    TP = x_prompt.shape[1]
    B = x_sample.shape[0]
    T = TP + B
    DT = D // P
    FT = ffn1_wdown.shape[1] // P
    WT = pool_scale.shape[1] // P
    BUF = state_pool.shape[2]
    CW = conv_w.shape[1]
    NMOD = w_ada.shape[2] // D
    HD = w_rg_a.shape[2]
    C = 1 + B
    ALPHA = (2 * DEPTH) ** 0.25
    EPS = 1e-5 / ALPHA ** 2
    LRU_C = 8.0
    assert (TP, DT, FT, WT, CW, HD, BUF) == (256, 8, 21, 4, 4, 64, 15)

    UP_UNITS, DOWN_UNITS, IN_UNITS, OUT_UNITS = FT, 12, 6, 6
    UNITS = 2 * (UP_UNITS + DOWN_UNITS) + IN_UNITS + OUT_UNITS
    UP = (0, UP_UNITS + DOWN_UNITS + IN_UNITS + OUT_UNITS)
    DOWN = (UP[0] + UP_UNITS, UP[1] + UP_UNITS)
    IN = DOWN[0] + DOWN_UNITS
    OUT = IN + IN_UNITS
    ROUNDS = UNITS // SLOTS
    assert UNITS % SLOTS == 0
    OUT_PLAN = [(0, 2, 0), (2, 3, 0), (5, 3, 0), (5, 3, 1), (2, 3, 1), (0, 2, 1)]
    S1, SC1, G1, S2, SC2, G2, S3, SC3, G3 = range(NMOD)
    CHUNKS = 4
    HALVES = 2
    PIECES = 4
    N_PARAM = 17

    with ExitStack() as ctx:
        def sb(name, shape, dt=F32, c=ctx):
            return c.enter_context(nc.sbuf_tensor(name, shape, dt))

        def sem(name):
            return ctx.enter_context(nc.semaphore(name))

        raw = sb("raw", [P, SLOTS, 16 * P])
        w_hi = sb("w_hi", [P, SLOTS, 16 * P], F32R)
        w_lo = sb("w_lo", [P, SLOTS, 16 * P], F32R)
        ada_raw = sb("ada_raw", [P, ADA_SLOTS, DT // 2, D // 2])
        x = sb("x", [P, DT, T])
        z = sb("z", [P, DT, T])
        m_hi = sb("m_hi", [P, DT, T], F32R)
        m_lo = sb("m_lo", [P, DT, T], F32R)
        with ExitStack() as c1:
            h_hi = sb("h_hi", [P, FT, T], F32R, c1)
            h_lo = sb("h_lo", [P, FT, T], F32R, c1)
        with ExitStack() as c2:
            win_a = sb("win_a", [P, WT, BUF + T], c=c2)
            win_b = sb("win_b", [P, WT, BUF + T], c=c2)
            up = sb("up", [P, WT, BUF + T], c=c2)
            ul = sb("ul", [P, WT, CW - 1 + T], c=c2)
            xc = sb("xc", [P, WT, T], c=c2)
            rg = sb("rg", [P, WT, T], c=c2)
            ig = sb("ig", [P, WT, T], c=c2)
            av = sb("av", [P, WT, T], c=c2)
            tt = sb("tt", [P, WT, T], c=c2)
            hs = sb("hs", [P, WT, T], c=c2)
        with ExitStack() as c3:
            sq = sb("sq", [P, DT, T], c=c3)
        with ExitStack() as c4:
            x_rows = sb("x_rows", [P, TP // P, D], c=c4)
            xs_rows = sb("xs_rows", [B, D], c=c4)
            c_rows = sb("c_rows", [C, D], c=c4)
            ys_rows = sb("ys_rows", [B, D], c=c4)
        sb("region_h", [P, 2 * FT * T])
        gate_act = sb("gate_act", [P, T])
        h_full = sb("h_full", [P, T])
        zsum = sb("zsum", [P, T])
        rstd = sb("rstd", [P, T])
        part = sb("part", [P, HALVES, P])
        coef = sb("coef", [P, 2, DT, C])
        last_ln = sb("last_ln", [P, 2, DT])
        spare = sb("spare", [P, 1])
        mod = sb("mod", [P, NMOD, DT, C])
        cT = sb("cT", [P, DT, 32])
        ident = sb("ident", [P, P])
        mean_w = sb("mean_w", [P, P])
        eps = sb("eps", [P, 1])
        credits = sb("credits", [P, 16])
        inv_head = sb("inv_head", [P, WT, 16])
        p_rows = sb("p_rows", [P, P])
        q_rows = sb("q_rows", [P, P])
        s_rows = sb("s_rows", [P, WT * P])
        r_rows = sb("r_rows", [32, WT * P])
        pT = sb("pT", [P, NMOD * DT + 6 * DT])
        qT = sb("qT", [P, 9 * WT])
        sp = sb("sp", [P, 10, WT])
        us = sb("us", [P, WT, B, BUF + 1])
        uls = sb("uls", [P, WT, B, CW])
        prod = sb("prod", [P, WT, B, CW])
        small = sb("small", [P, WT, B])
        h0 = sb("h0", [P, WT, B])
        wp = sb("wp", [P, WT, P])
        wg = sb("wg", [P, 2, WT, P])
        bank = [ctx.enter_context(nc.psum_tensor(f"bank{i}", [P, 512], F32)) for i in range(8)]
        ADA_PART = (6, 7)
        ADA_OUT = [(6, 6)] * NMOD
        ADA_OUT[S1], ADA_OUT[SC1] = (3, 3), (6, 5)
        MEAN, VAR = 4, 5
        GATES = ((0, 0, 4), (0, 1, 5), (1, 0, 0), (1, 1, 1), (0, 2, 2), (0, 3, 3), (1, 2, 0), (1, 3, 1))

        bias_mod = pT[:, 0:NMOD * DT].rearrange("p (v m) -> p v m", v=NMOD)
        ln_gT = pT[:, NMOD * DT:NMOD * DT + 3 * DT].rearrange("p (v m) -> p v m", v=3)
        ln_bT = pT[:, NMOD * DT + 3 * DT:NMOD * DT + 6 * DT].rearrange("p (v m) -> p v m", v=3)
        pscT, cbT, baT, bxT, lamT = (qT[:, WT * i:WT * (i + 1)] for i in (0, 5, 6, 7, 8))
        cwT = qT[:, WT:5 * WT].rearrange("p (k m) -> p k m", k=CW)
        c8, nc8 = sp[:, 0], sp[:, 1]

        x_landed = sem("x_landed")
        c_landed = sem("c_landed")
        param_landed = sem("param_landed")
        w_landed = [sem(f"w_landed{i}") for i in range(SLOTS)]
        ada_landed = [sem(f"ada_landed{i}") for i in range(ADA_SLOTS)]
        stored = sem("stored")
        y_stored = sem("y_stored")
        consts = sem("consts")
        lo_split = sem("lo_split")
        units_done = sem("units_done")
        gate_read = sem("gate_read")
        up_read = sem("up_read")
        pair_read = sem("pair_read")
        ada_used = sem("ada_used")
        hi_split = sem("hi_split")
        gate_done = sem("gate_done")
        h_hi_done = sem("h_hi_done")
        h_ready = sem("h_ready")
        m_full = sem("m_full")
        m_hi_done = sem("m_hi_done")
        m_ready = sem("m_ready")
        part_ready = sem("part_ready")
        mod_out = sem("mod_out")
        half_out = sem("half_out")
        mod_read = sem("mod_read")
        prep_out = sem("prep_out")
        prep_read = sem("prep_read")
        sums_ready = sem("sums_ready")
        stat_out = sem("stat_out")
        centred = sem("centred")
        squared = sem("squared")
        std_ready = sem("std_ready")
        normed = sem("normed")
        x_scaled = sem("x_scaled")
        x_ready = sem("x_ready")
        coef_ready = sem("coef_ready")
        sample_full = sem("sample_full")
        up_copied = sem("up_copied")
        ul_copied = sem("ul_copied")
        gates_read = sem("gates_read")
        gelu_done = sem("gelu_done")
        xc_ready = sem("xc_ready")
        gate_mm = sem("gate_mm")
        sig_done = sem("sig_done")
        pooled_ready = sem("pooled_ready")
        pool_mm = sem("pool_mm")
        ypool_done = sem("ypool_done")
        decay_done = sem("decay_done")
        ratio_ready = sem("ratio_ready")
        root_done = sem("root_done")
        ylru_done = sem("ylru_done")
        out_read = sem("out_read")
        rows_out = sem("rows_out")
        rows_ready = sem("rows_ready")
        c_silu = sem("c_silu")
        init_out = sem("init_out")
        init_read = sem("init_read")
        final_x = sem("final_x")
        fin_out = sem("fin_out")
        fin_read = sem("fin_read")
        lam_ready = sem("lam_ready")
        lam_exp = sem("lam_exp")
        vector_steps = sem("vector_steps")
        gu_view = [w.rearrange("l (k p) (h f c) -> l h f p k c", p=P, h=2, c=P) for w in (ffn1_wgu, ffn2_wgu)]
        down_view = [w.rearrange("l (t k p) (m c) -> l t m p k c", t=3, p=P, c=2 * P)
                     for w in (ffn1_wdown, ffn2_wdown)]
        in_view = w_in.rearrange("l (k p) (m c) -> l m p k c", p=P, c=2 * P)
        out_view = w_out.rearrange("l (k p) d -> l p k d", p=P)
        ada_view = w_ada.rearrange("l (s k p) (v h d) -> l v h s p k d", s=2, p=P, v=NMOD, h=HALVES)

        block = ctx.enter_context(nc.Block())

        @block.sync
        def _(sync):
            with sync.Fori(0, DEPTH) as l:
                def slot_free(unit):
                    sync.wait_ge(lo_split, l * UNITS + unit + 1)

                def load_unit(unit, slot, halves):
                    slot_free(unit)
                    for dst, src in halves:
                        sync.dma_start(dst, src).then_inc(w_landed[slot], 16)

                def tiles(slot, c):
                    return raw[:, slot].rearrange("p (k c) -> p k c", c=c)

                def load_gate_up(f, tile, unit, slot):
                    half = raw[:, slot].rearrange("p (h k c) -> p h k c", h=2, c=P)
                    load_unit(unit, slot, [(half[:, h], gu_view[f][l, h, tile]) for h in range(2)])

                def load_down(f, pair, third, unit):
                    dst, src = tiles(third, 2 * P), down_view[f][l, third, pair]
                    load_unit(unit, third, [(dst[:, 0:4], src[:, 0:4]), (dst[:, 4:7], src[:, 4:7])])

                def load_ada(v, chunks=range(CHUNKS)):
                    for c in chunks:
                        sync.wait_ge(ada_used, l * (NMOD * CHUNKS) + (v * CHUNKS + c + 1))
                        sync.dma_start(ada_raw[:, c], ada_view[l, v, c // 2, c % 2]).then_inc(ada_landed[c], 16)

                def load_gate_ups(f, first, end=UP_UNITS // SLOTS):
                    with sync.Fori(first, end) as r:
                        for j in range(SLOTS):
                            load_gate_up(f, r * SLOTS + j, r * SLOTS + (UP[f] + j), j)

                def load_downs(f, first=0, end=DOWN_UNITS // SLOTS):
                    with sync.Fori(first, end) as pair:
                        for third in range(3):
                            load_down(f, pair, third, pair * SLOTS + (DOWN[f] + third))

                load_ada(S1)
                load_gate_up(0, 0, 0, 0)
                load_ada(SC1)
                load_gate_up(0, 1, 1, 1)
                load_gate_up(0, 2, 2, 2)
                for r in range(1, 1 + CHUNKS):
                    for j in range(SLOTS):
                        load_gate_up(0, r * SLOTS + j, r * SLOTS + j, j)
                    load_ada(G1, (r - 1,))
                load_gate_ups(0, 1 + CHUNKS)
                load_downs(0, 0, 2)
                load_ada(S2)
                load_downs(0, 2)
                load_ada(SC2)
                for i in range(IN_UNITS):
                    if i == 3:
                        load_ada(G2)
                    dst = tiles(i % SLOTS, 2 * P)
                    load_unit(IN + i, i % SLOTS, [(dst[:, 4 * k:4 * k + 4], in_view[l, i, :, 4 * k:4 * k + 4])
                                                  for k in range(2)])
                for i, (m, n, kh) in enumerate(OUT_PLAN):
                    if i == 3:
                        load_ada(S3)
                    if i == 4:
                        load_ada(SC3, (0, 1))
                    dst = raw[:, i % SLOTS, 0:4 * n * P].rearrange("p (k c) -> p k c", c=n * P)
                    load_unit(OUT + i, i % SLOTS,
                              [(dst[:, 2 * k:2 * k + 2],
                                out_view[l, :, 4 * kh + 2 * k:4 * kh + 2 * k + 2, m * P:(m + n) * P])
                               for k in range(2)])
                load_ada(SC3, (2, 3))
                for j in range(SLOTS):
                    load_gate_up(1, j, UP[1] + j, j)
                load_ada(G3)
                load_gate_ups(1, 1)
                load_downs(1)

            y_view = y_prompt.rearrange("o (a p) d -> p (o a) d", p=P)
            for a in (0, D // 2):
                sync.wait_ge(fin_read, 2 * ((a + D // 2) // P))
                sync.dma_start(y_view[:, :, a:a + D // 2], x_rows[:, :, a:a + D // 2]).then_inc(y_stored, 16)
            sync.dma_start(y_sample.rearrange("b o d -> (b o) d"), ys_rows[:]).then_inc(y_stored, 16)
            sync.wait_ge(y_stored, 48)

        @block.gpsimd
        def _(pool):
            pool.memset(ident[:], 0.0).then_inc(consts, 1)
            pool.memset(mean_w[:], 1.0 / D).then_inc(consts, 1)
            pool.memset(cT[:], 0.0).then_inc(consts, 1)
            pool.memset(eps[:], EPS).then_inc(consts, 1)
            pool.memset(wg[:], 0.0).then_inc(consts, 1)
            for g, w in enumerate(WINDOWS):
                pool.memset(inv_head[:, g, w - 1:16], 1.0 / w).then_inc(consts, 1)
                for t in range(w - 1):
                    pool.memset(inv_head[:, g, t:t + 1], 1.0 / (t + 1)).then_inc(consts, 1)
            n = 5 + WT + sum(w - 1 for w in WINDOWS)
            pool.wait_ge(consts, n)
            pool.affine_select(out=ident[:], in_=ident[:], compare_op=ALU.not_equal, fill=1.0, base=0,
                               pattern=[[-1, P]], channel_multiplier=1).then_inc(consts, 1)
            for k, (s, credit) in enumerate(((lo_split, SLOTS), (units_done, SLOTS), (gate_read, 3), (up_read, 3),
                                             (pair_read, 2), (ada_used, ADA_SLOTS), (part_ready, 2),
                                             (mod_read, 1), (h_ready, 1))):
                pool.memset(credits[:, k:k + 1], 0.0).then_inc(s, credit)

            with pool.Fori(0, DEPTH) as l:
                def load(dst, src):
                    pool.dma_start(dst, src).then_inc(param_landed, 16)

                lw = lambda a: a[l].rearrange("(r c) -> r c", c=P)
                nb, nl = NMOD * DT, 3 * DT
                load(p_rows[0:nb, :], lw(b_ada))
                load(p_rows[nb:nb + nl, :], ln_g[l].rearrange("i (r c) -> (i r) c", c=P))
                load(p_rows[nb + nl:nb + 2 * nl, :], ln_b[l].rearrange("i (r c) -> (i r) c", c=P))
                load(q_rows[0:WT, :], lw(pool_scale))
                load(q_rows[WT:5 * WT, :], conv_w[l].rearrange("k (r c) -> (k r) c", c=P))
                for i, a in ((5, conv_b), (6, b_rg_a), (7, b_rg_x), (8, lru_lambda)):
                    load(q_rows[i * WT:(i + 1) * WT, :], lw(a))
                load(s_rows[0:B * BUF, :], state_pool[l].rearrange("b t d -> (b t) d"))
                load(r_rows[0:B * (CW - 1), :], state_conv[l].rearrange("b t d -> (b t) d"))
                load(r_rows[24:24 + B, :], state_rglru[l])
                load(wp[:], w_pool[l].rearrange("g c d -> c g d"))
                for k, a in enumerate((w_rg_a, w_rg_x)):
                    for e in range(2):
                        heads = a[l].rearrange("(m e) i j -> e i m j", e=2)[e]
                        load(wg[HD * e:HD * (e + 1), k, :, HD * e:HD * (e + 1)], heads)
                pool.dma_start(pool_sample[l, :, 0:BUF - 1], state_pool[l, :, 1:BUF]).then_inc(stored, 16)
                pool.dma_start(conv_sample[l, :, 0:CW - 2], state_conv[l, :, 1:CW - 1]).then_inc(stored, 16)
                for i, (g, b) in enumerate(((last_ln[:, 0], last_ln[:, 1]), (ln_gT[:, 0], ln_bT[:, 0]),
                                            (ln_gT[:, 1], ln_bT[:, 1]))):
                    if i == 1:
                        pool.wait_ge(prep_read, l * 2 + 2)
                    wide = lambda a: a[:, m:m + 1].broadcast_to([P, T])
                    for m in range(DT):
                        pool.wait_ge(normed, l * (3 * DT) + (i * DT + m + 1))
                        pool.tensor_tensor(x[:, m], z[:, m], wide(g), ALU.mult).then_inc(x_scaled, 1)
                    for m in range(DT):
                        pool.wait_ge(x_scaled, l * (3 * DT) + (i * DT + m + 1))
                        pool.tensor_tensor(x[:, m], x[:, m], wide(b), ALU.add).then_inc(x_ready, 1)
                pool.wait_ge(rows_ready, (l + 1) * 3)
                for dst, a, b in ((pool_prompt[l, 0], 0, BUF), (pool_sample[l, :, BUF - 1], BUF, BUF + B),
                                  (conv_prompt[l, 0], 32, 32 + CW - 1),
                                  (conv_sample[l, :, CW - 2], 32 + CW - 1, 32 + CW - 1 + B),
                                  (h_prompt[l], 64, 65), (h_sample[l], 65, 65 + B)):
                    pool.dma_start(dst, s_rows[a:b, :]).then_inc(stored, 16)
                pool.wait_ge(stored, (l + 1) * (8 * 16))

        @block.tensor
        def _(pe):
            def transpose_rows(out, rows):
                return pe.transpose(out, rows, ident[0:rows.shape[0], 0:rows.shape[0]])

            pe.wait_ge(consts, 6 + WT + sum(w - 1 for w in WINDOWS))
            pe.wait_ge(c_silu, 1)
            for m in range(DT):
                t = transpose_rows(bank[0][:, m * C:(m + 1) * C], c_rows[:, m * P:(m + 1) * P])
            t.then_inc(init_out, 1)
            pe.wait_ge(x_landed, 32)
            for m in range(DT):
                b = bank[1 + m % 4]
                if m >= 4:
                    pe.wait_ge(normed, m - 3)
                for a in range(TP // P):
                    transpose_rows(b[:, a * P:(a + 1) * P], x_rows[:, a, m * P:(m + 1) * P])
                transpose_rows(b[:, TP:T], xs_rows[:, m * P:(m + 1) * P]).then_inc(init_out, 1)
            pe.wait_ge(init_read, 1)
            pe.wait_ge(normed, DT)

            def layer(l):
                def unit_ready(unit):
                    pe.wait_ge(lo_split, l * UNITS + unit + (1 + SLOTS))

                def product(out, hi, lo, r_hi, r_lo, start, stop, done=None):
                    pe.matmul(out, hi, r_hi, start=start, stop=False)
                    pe.matmul(out, hi, r_lo, start=False, stop=False)
                    mm = pe.matmul(out, lo, r_hi, start=False, stop=stop)
                    if stop and done is not None:
                        mm.then_inc(done, 1)
                    return mm

                def weight(slot, i):
                    return w_hi[:, slot, i * P:(i + 1) * P], w_lo[:, slot, i * P:(i + 1) * P]

                def ada_part(v, h):
                    if h == 0 and v != SC1:
                        pe.wait_ge(mod_read, l * NMOD + (v + 1))
                    pe.wait_ge(part_ready, l * (NMOD * HALVES) + (v * HALVES + h + 1))
                    for k in range(DT):
                        c = 2 * h + k // 4
                        if k % 4 == 0:
                            pe.wait_ge(ada_landed[c], (l * NMOD + (v + 1)) * 16)
                        for g in range(4):
                            mm = pe.matmul(bank[ADA_PART[h]][32 * g:32 * g + 32, 0:P], cT[:, k, :],
                                           ada_raw[:, c, k % 4, g * P:(g + 1) * P], start=k == 0, stop=k == DT - 1,
                                           tile_position=(0, 32 * g))
                        if k % 4 == 3:
                            mm.then_inc(ada_used, 1)

                def ada_turn(v, h):
                    pe.wait_ge(part_ready, l * (NMOD * HALVES) + (v * HALVES + h + 3))
                    mm = pe.transpose(bank[ADA_OUT[v][h]][:, (h + 1) * P:(h + 2) * P], part[:, h], ident[:])
                    if h:
                        mm.then_inc(mod_out, 1)
                    elif v == SC1:
                        mm.then_inc(half_out, 1)

                def ada_rest(v):
                    ada_part(v, 1)
                    ada_turn(v, 0)
                    ada_turn(v, 1)

                def ada(v):
                    ada_part(v, 0)
                    ada_rest(v)

                def mean(i):
                    pe.wait_ge(sums_ready, l * 3 + (i + 1))
                    pe.matmul(bank[MEAN][:, 0:T], mean_w[:], zsum[:], start=True, stop=True).then_inc(stat_out, 1)

                def variance(i):
                    for m in range(DT):
                        if m % 2 == 0:
                            pe.wait_ge(squared, l * (3 * DT // 2) + (i * DT // 2 + m // 2 + 1))
                        mm = pe.matmul(bank[VAR][:, 0:T], mean_w[:], sq[:, m], start=m == 0, stop=m == DT - 1)
                    mm.then_inc(stat_out, 1)

                def turn_rows():
                    for b, src, a, n in ((2, up, TP, BUF + B), (3, ul, TP, CW - 1 + B), (4, hs, TP - 1, 1 + B)):
                        for m in range(WT):
                            t = pe.transpose(bank[b][0:n, m * P:(m + 1) * P], src[:, m, a:a + n], ident[:])
                        t.then_inc(rows_out, 1)

                def norm_beside(i, v, after):
                    ada_part(v, 0)
                    mean(i)
                    ada_rest(v)
                    variance(i)
                    ada_part(after, 0)
                    if i == 1:
                        turn_rows()
                    ada_part(after, 1)

                def keep_warm(n):
                    for _ in range(n):
                        pe.matmul(bank[ADA_PART[1]][:, 0:P], ident[:], ident[:], start=True, stop=True)

                def inputs_ready(first, k):
                    pe.wait_ge(m_ready, l * (3 * DT + 2) + (first + k + 1))

                def down_pair(f, pair, gate):
                    for third in range(3):
                        unit_ready(DOWN[f] + 3 * pair + third)
                        pe.wait_ge(h_ready, l * (2 * FT) + (f * FT + 7 * (third + 1) + 1))
                        if third == 0:
                            pe.wait_ge(up_read, l * (2 * FT) + (f * FT + FT - 2 + min(pair, 1) + 3))
                            pe.wait_ge(pair_read, l * 8 + (f * 4 + pair + 1))
                        for i in range(2):
                            for k in range(7):
                                mm = product(bank[2 * (pair % 2) + i][:, 0:T], *weight(third, 2 * k + i),
                                             h_hi[:, 7 * third + k], h_lo[:, 7 * third + k],
                                             third == 0 and k == 0, third == 2 and k == 6)
                        mm.then_inc(units_done, 1)
                        if pair == 0 and third == 0:
                            ada_turn(gate, 0)
                            ada_turn(gate, 1)

                def feed_forward(f, vectors):
                    with pe.Fori(0, UP_UNITS // SLOTS) as r:
                        for j in range(SLOTS):
                            if j == 0 and f == 0:
                                pe.wait_ge(prep_read, l * 2 + 2)
                            if j == 1 and f == 1:
                                pe.wait_ge(rows_ready, l * 3 + 3)
                            unit_ready(r * SLOTS + (UP[f] + j))
                            turn = l * (2 * FT) + r * SLOTS + (f * FT + j + 1)
                            pe.wait_ge(gate_read, turn)
                            if j == 0:
                                pe.wait_ge(up_read, turn)
                                for k in range(DT):
                                    inputs_ready(f * (2 * DT + 2), k)
                                    product(bank[2 * j][:, 0:T], *weight(j, k), m_hi[:, k], m_lo[:, k],
                                            k == 0, k == DT - 1, gate_done)
                                    product(bank[2 * j + 1][:, 0:T], *weight(j, DT + k), m_hi[:, k], m_lo[:, k],
                                            k == 0, k == DT - 1, units_done)
                                continue
                            for k in range(DT):
                                product(bank[2 * j][:, 0:T], *weight(j, k), m_hi[:, k], m_lo[:, k],
                                        k == 0, k == DT - 1, gate_done)
                            pe.wait_ge(up_read, turn)
                            for k in range(DT):
                                product(bank[2 * j + 1][:, 0:T], *weight(j, DT + k), m_hi[:, k], m_lo[:, k],
                                        k == 0, k == DT - 1, units_done)
                    if f == 0:
                        ada_part(vectors[0], 0)
                        ada_part(vectors[0], 1)
                    for pair in range(4):
                        down_pair(f, pair, vectors[0])
                        if pair == 1 and len(vectors) > 1:
                            ada(vectors[1])

                ada(S1)
                ada_part(SC1, 0)
                pe.wait_ge(param_landed, (l + 1) * (16 * N_PARAM))
                for m in range(WT):
                    transpose_rows(bank[0][:, m * 120:(m + 1) * 120], s_rows[0:B * BUF, m * P:(m + 1) * P])
                for m in range(WT):
                    transpose_rows(bank[1][:, m * 32:(m + 1) * 32], r_rows[:, m * P:(m + 1) * P])
                transpose_rows(bank[1][:, 128:248], p_rows[0:120, :])
                transpose_rows(bank[1][:, 248:284], q_rows[0:36, :]).then_inc(prep_out, 1)
                ada_turn(SC1, 0)
                ada_part(SC1, 1)
                ada_turn(SC1, 1)
                feed_forward(0, [G1, S2])
                norm_beside(0, SC2, G2)

                def recurrence_gates():
                    pe.wait_ge(gates_read, l * 2 + 1)
                    for i, (kind, m, b) in enumerate(GATES):
                        if i in (0, 4):
                            pe.wait_ge(xc_ready, l * 2 + i // 4 + 1)
                        if i >= 6:
                            pe.wait_ge(sig_done, l * (2 * WT) + i - 3)
                        pe.matmul(bank[b][:, 0:T], wg[:, kind, m, :], xc[:, m, :],
                                  start=True, stop=True).then_inc(gate_mm, 1)

                for u in range(IN_UNITS):
                    if u == 1:
                        ada_turn(G2, 0)
                        ada_turn(G2, 1)
                    if u == 5:
                        recurrence_gates()
                        pe.wait_ge(sig_done, l * (2 * WT) + 2)
                    unit_ready(IN + u)
                    if u in (3, 4):
                        pe.wait_ge(up_copied, l * 2 + (u - 2))
                    steps = [(i, k) for i in range(2) for k in range(DT)]
                    if u == 0:
                        steps.sort(key=lambda step: step[1])
                    for i, k in steps:
                        if u == 0 and i == 0:
                            inputs_ready(DT, k)
                        mm = product(bank[2 * (u % 3) + i][:, 0:T], *weight(u % SLOTS, 2 * k + i),
                                     m_hi[:, k], m_lo[:, k], k == 0, k == DT - 1)
                    mm.then_inc(units_done, 1)
                pe.wait_ge(pooled_ready, l + 1)
                pe.wait_ge(sig_done, (l + 1) * (2 * WT))
                for g in range(WT):
                    pe.matmul(bank[g][:, 0:T], wp[:, g, :], z[:, g, :], start=True, stop=True)\
                      .then_inc(pool_mm, 1)
                ada_part(S3, 0)
                ada_part(S3, 1)

                pe.wait_ge(ypool_done, l * WT + WT)
                pe.wait_ge(gates_read, l * 2 + 2)
                for i, (m0, n, kh) in enumerate(OUT_PLAN):
                    unit_ready(OUT + i)
                    if i == 1:
                        ada_turn(S3, 0)
                        ada_turn(S3, 1)
                    if i == 2:
                        pe.wait_ge(mod_read, l * NMOD + (S3 + 2))
                    if i % 3 == 0:
                        inputs_ready(2 * DT, kh)
                    for m in range(n):
                        for k in range(4):
                            mm = product(bank[m0 + m][:, 0:T], *weight(i % SLOTS, k * n + m),
                                         m_hi[:, 4 * kh + k], m_lo[:, 4 * kh + k],
                                         kh == 0 and k == 0, kh == 1 and k == 3)
                    mm.then_inc(units_done, 1)

                pe.wait_ge(out_read, l * 3 + 1)
                norm_beside(1, SC3, G3)
                feed_forward(1, [G3])
                keep_warm(8)
                mean(2)
                keep_warm(6)
                variance(2)

            with pe.Fori(0, DEPTH) as l:
                layer(l)

            for m in range(DT):
                pe.wait_ge(final_x, m + 1)
                b = bank[m]
                for a in range(TP // P):
                    pe.transpose(b[:, a * P:(a + 1) * P], x[:, m, a * P:(a + 1) * P], ident[:])
                pe.transpose(b[0:B, TP:TP + P], x[:, m, TP:T], ident[:]).then_inc(fin_out, 1)

        @block.scalar
        def _(act):
            act.dma_start(c_rows[0:1, :], c_prompt).then_inc(c_landed, 16)
            act.dma_start(c_rows[1:C, :], c_sample).then_inc(c_landed, 16)
            act.dma_start(xs_rows[:], x_sample.rearrange("b o d -> (b o) d")).then_inc(x_landed, 16)
            act.dma_start(x_rows[:], x_prompt.rearrange("o (a p) d -> p (o a) d", p=P)).then_inc(x_landed, 16)
            act.wait_ge(c_landed, 32)
            act.activation(c_rows[:], c_rows[:], ACT.Silu).then_inc(c_silu, 1)

            def layer(l):
                def split(unit, rounds, slot):
                    act.wait_ge(w_landed[slot], (l * ROUNDS + rounds + 1) * 32)
                    act.wait_ge(units_done, l * UNITS + unit + 1)
                    act.activation(w_hi[:, slot], raw[:, slot], ACT.Copy).then_inc(hi_split, 1)

                def split_at(unit):
                    split(unit, unit // SLOTS, unit % SLOTS)

                def ada_copy(v, halves=(0, 1)):
                    for h in halves:
                        act.wait_ge(ada_used, l * (NMOD * CHUNKS) + (v * CHUNKS + 2 * h + 2 + ADA_SLOTS))
                        act.activation(part[:, h], bank[ADA_PART[h]][:, 0:P], ACT.Copy).then_inc(part_ready, 1)

                def norm(i, v):
                    act.activation(spare[:], eps[:], ACT.Sqrt)
                    if v is not None:
                        ada_copy(v, (0,))
                    for g in range(DT // 2):
                        act.wait_ge(centred, l * (3 * DT // 2) + (i * DT // 2 + g + 1))
                        act.activation(sq[:, 2 * g:2 * g + 2], z[:, 2 * g:2 * g + 2], ACT.Square).then_inc(squared, 1)
                    if v is not None:
                        ada_copy(v, (1,))
                    act.wait_ge(stat_out, l * 6 + (2 * i + 2))
                    act.activation(rstd[:], bank[VAR][:, 0:T], ACT.Sqrt, bias=eps[:]).then_inc(std_ready, 1)

                def modulate(i, piece, m0=0, n=DT):
                    def full(m):
                        act.wait_ge(normed, l * (3 * DT) + (i * DT + m + 1))
                        act.activation(sq[:, m, 0:TP], z[:, m, 0:TP], ACT.Identity, scale=coef[:, 0, m, 0:1],
                                       bias=coef[:, 1, m, 0:1]).then_inc(m_full, 1)

                    def high(m):
                        act.wait_ge(m_full, l * (3 * DT) + (i * DT + m + 1))
                        act.activation(m_hi[:, m], sq[:, m], ACT.Copy).then_inc(m_hi_done, 1)

                    act.wait_ge(coef_ready, l * PIECES + (piece + 1))
                    full(m0)
                    act.wait_ge(sample_full, l * PIECES + (piece + 1))
                    high(m0)
                    full(m0 + 1)
                    for m in range(m0 + 2, m0 + n):
                        full(m)
                        high(m - 1)
                    high(m0 + n - 1)

                def feed_forward(f, vectors):
                    with act.Fori(0, UP_UNITS // SLOTS) as r:
                        for j in range(SLOTS):
                            n = UP[f] + j + 2
                            split(r * SLOTS + n, r + n // SLOTS, n % SLOTS)
                            turn = l * (2 * FT) + r * SLOTS + (f * FT + j + 1)
                            act.wait_ge(gate_done, turn)
                            act.activation(gate_act[:], bank[2 * j][:, 0:T], ACT.Silu).then_inc(gate_read, 1)
                            act.wait_ge(up_read, turn + 3)
                            act.activation(h_hi[:, r * SLOTS + j], h_full[:], ACT.Copy).then_inc(h_hi_done, 1)
                    ada_copy(vectors[0])
                    for i in range(DOWN_UNITS - (2 if f else 0)):
                        split_at(DOWN[f] + i + 2)
                        if i == 1 and f == 0:
                            act.wait_ge(lam_ready, l + 1)
                            act.activation(sp[:, 4], sp[:, 3], ACT.Exp).then_inc(lam_exp, 1)
                        if i == 5 and len(vectors) > 1:
                            ada_copy(vectors[1])

                ada_copy(S1)
                split_at(0)
                ada_copy(SC1, (0,))
                modulate(0, 0, 0, 4)
                ada_copy(SC1, (1,))
                modulate(0, 1, 4, 4)
                split_at(1)
                feed_forward(0, [G1, S2])
                norm(0, SC2)
                modulate(1, 2)
                for i in range(IN_UNITS):
                    if i == 1:
                        ada_copy(G2)
                    if i < 5:
                        split_at(IN + i + 2)
                    if i in (2, 3):
                        act.wait_ge(units_done, l * UNITS + IN + i + 1 + SLOTS)
                        for j in range(2):
                            o = act.activation(ul[:, 2 * (i - 2) + j, CW - 1:CW - 1 + T],
                                               bank[2 * (i % 3) + j][:, 0:T], ACT.Copy)
                        o.then_inc(ul_copied, 1)
                    if i >= 4:
                        act.wait_ge(x_ready, l * (3 * DT) + 2 * DT)
                        act.wait_ge(units_done, l * UNITS + IN + i + 1 + SLOTS)
                        for j in range(2):
                            o = act.activation(z[:, WT + 2 * (i - 4) + j], bank[2 * (i % 3) + j][:, 0:T],
                                               ACT.Copy)
                        o.then_inc(gates_read, 1)
                    if i == 4:
                        for n, (kind, m, gate_bank) in enumerate(GATES):
                            act.wait_ge(gate_mm, l * (2 * WT) + n + 1)
                            dst, b = ((rg, baT), (ig, bxT))[kind]
                            act.activation(dst[:, m], bank[gate_bank][:, 0:T], ACT.Sigmoid,
                                           bias=b[:, m:m + 1]).then_inc(sig_done, 1)
                        act.wait_ge(sig_done, (l + 1) * (2 * WT))
                        for m in range(WT):
                            act.activation(tt[:, m], rg[:, m], ACT.Tanh, scale=c8[:, m:m + 1])\
                               .then_inc(decay_done, 1)
                        for m in range(WT):
                            act.activation(av[:, m], rg[:, m], ACT.Exp, scale=nc8[:, m:m + 1])\
                               .then_inc(decay_done, 1)
                for g in range(WT):
                    act.wait_ge(pool_mm, l * WT + g + 1)
                    act.activation(z[:, g], bank[g][:, 0:T], ACT.Copy, scale=pscT[:, g:g + 1])\
                       .then_inc(ypool_done, 1)
                act.wait_ge(ypool_done, (l + 1) * WT)
                act.activation(m_hi[:, 0:WT], z[:, 0:WT], ACT.Copy).then_inc(m_hi_done, 1)
                split_at(OUT + 1)
                ada_copy(S3, (0,))
                act.wait_ge(ratio_ready, l + 1)
                act.activation(rg[:], tt[:], ACT.Sqrt).then_inc(root_done, 1)
                ada_copy(S3, (1,))
                split_at(OUT + 2)
                act.wait_ge(gates_read, l * 2 + 2)
                act.activation(z[:, WT:], z[:, WT:], ACT.Gelu_apprx_tanh).then_inc(gelu_done, 1)
                split_at(OUT + 3)
                act.wait_ge(ylru_done, l + 1)
                act.activation(m_hi[:, WT:], z[:, WT:], ACT.Copy).then_inc(m_hi_done, 1)
                for i in range(2, OUT_UNITS):
                    split_at(OUT + i + 2)
                norm(1, SC3)
                modulate(2, 3)
                feed_forward(1, [G3])
                norm(2, None)

            with act.Fori(0, DEPTH) as l:
                layer(l)

            for m in range(DT):
                act.wait_ge(normed, DEPTH * (3 * DT) + m + 1)
                act.activation(x[:, m], z[:, m], ACT.Identity, scale=ln_gT[:, 2, m:m + 1],
                               bias=ln_bT[:, 2, m:m + 1]).then_inc(final_x, 1)

        @block.vector
        def _(dve):
            own = Own(dve, vector_steps)
            n_consts = 6 + WT + sum(w - 1 for w in WINDOWS)
            dve.wait_ge(consts, n_consts)
            own.did(dve.memset(last_ln[:, 0], 1.0))
            own.did(dve.memset(last_ln[:, 1], 0.0))
            dve.wait_ge(init_out, 1)
            dve.tensor_copy(cT[:, :, 0:C], bank[0][:, 0:DT * C].rearrange("p (m c) -> p m c", c=C))\
               .then_inc(init_read, 1)
            for m in range(DT):
                dve.wait_ge(init_out, 2 + m)
                dve.tensor_copy(z[:, m], bank[1 + m % 4][:, 0:T]).then_inc(normed, 1)
            prologue = own.n

            def layer(l):
                own.base, own.n = l * VECTOR_STEPS + prologue, 0

                def split(unit, slot):
                    dve.wait_ge(hi_split, l * UNITS + unit + 1)
                    dve.tensor_tensor(w_lo[:, slot], raw[:, slot], w_hi[:, slot].bitcast(F32), ALU.subtract)\
                       .then_inc(lo_split, 1)

                def half_turned(v, h):
                    return bank[ADA_OUT[v][h]][:, (h + 1) * P:(h + 2) * P]\
                        .rearrange("p (m c) -> p m c", c=32)[:, :, 0:C]

                def bias(v, m0, n):
                    return bias_mod[:, v, m0:m0 + n].unsqueeze(2).broadcast_to([P, n, C])

                def finish_vector(v):
                    dve.wait_ge(mod_out, l * NMOD + (v + 1))
                    if v == SC1:
                        dve.tensor_tensor(mod[:, v, 4:8], half_turned(v, 1), bias(v, 4, 4), ALU.add)\
                           .then_inc(mod_read, 1)
                    else:
                        both = bank[ADA_OUT[v][0]][:, P:3 * P].rearrange("p (m c) -> p m c", c=32)[:, :, 0:C]
                        dve.tensor_tensor(mod[:, v], both, bias(v, 0, DT), ALU.add).then_inc(mod_read, 1)
                    if v in (G1, G2, G3):
                        factor = (1.0 if v == G2 else 0.5) / ALPHA
                        dve.wait_ge(mod_read, l * NMOD + (v + 2))
                        own.did(dve.tensor_scalar(mod[:, v], mod[:, v], factor, factor, ALU.mult, ALU.add))

                def coefficients(shift, scale, g, b, m0=0, n=DT):
                    own.wait()
                    t = slice(m0, m0 + n)
                    g, b = (a[:, t].unsqueeze(2).broadcast_to([P, n, C]) for a in (g, b))
                    own.then(dve.tensor_tensor(coef[:, 1, t], mod[:, scale, t], b, ALU.mult))
                    own.did(dve.tensor_tensor(coef[:, 1, t], coef[:, 1, t], mod[:, shift, t], ALU.add))
                    dve.tensor_tensor(coef[:, 0, t], mod[:, scale, t], g, ALU.mult).then_inc(coef_ready, 1)

                def modulate_samples(piece, m0=0, n=DT):
                    t = slice(m0, m0 + n)
                    dve.wait_ge(coef_ready, l * PIECES + (piece + 1))
                    own.then(dve.tensor_tensor(sq[:, t, TP:T], z[:, t, TP:T], coef[:, 0, t, 1:C], ALU.mult))
                    dve.tensor_tensor(sq[:, t, TP:T], sq[:, t, TP:T], coef[:, 1, t, 1:C], ALU.add)\
                       .then_inc(sample_full, 1)

                def split_input(i, m0=0, n=DT):
                    for m in range(m0, m0 + n):
                        dve.wait_ge(m_hi_done, l * (3 * DT + 2) + (m + 1 + (0, DT, 2 * DT + 2)[i]))
                        dve.tensor_tensor(m_lo[:, m], sq[:, m], m_hi[:, m].bitcast(F32), ALU.subtract)\
                           .then_inc(m_ready, 1)

                def residual(tiles, gate, read, first, last):
                    own.wait()
                    for m, b in tiles:
                        dve.wait_ge(x_ready, l * (3 * DT) + ({G1: 0, G2: DT, G3: 2 * DT}[gate] + m + 1))
                        own.did(dve.scalar_tensor_tensor(z[:, m, 0:TP], bank[b][:, 0:TP], mod[:, gate, m, 0:1],
                                                         x[:, m, 0:TP], ALU.mult, ALU.add))
                        o = dve.tensor_tensor(z[:, m, TP:T], bank[b][:, TP:T], mod[:, gate, m, 1:C], ALU.mult)
                        if (m, b) != tiles[-1]:
                            own.did(o)
                    o.then_inc(read[0], 1)
                    dve.wait_ge(*read)
                    m0, n = tiles[0][0], len(tiles)
                    own.then(dve.tensor_tensor(z[:, m0:m0 + n, TP:T], z[:, m0:m0 + n, TP:T],
                                               x[:, m0:m0 + n, TP:T], ALU.add))
                    for m, _ in tiles:
                        if m == first:
                            own.then(dve.tensor_copy(zsum[:], z[:, m]))
                        elif m != last:
                            own.then(dve.tensor_tensor(zsum[:], zsum[:], z[:, m], ALU.add))
                        else:
                            dve.tensor_tensor(zsum[:], zsum[:], z[:, m], ALU.add).then_inc(sums_ready, 1)

                def norm(i, shift=None, scale=None, units=()):
                    dve.wait_ge(stat_out, l * 6 + (2 * i + 1))
                    for g in range(DT // 2):
                        a = 2 * g
                        dve.tensor_tensor(z[:, a:a + 2], z[:, a:a + 2],
                                          bank[MEAN][:, 0:T].unsqueeze(1).broadcast_to([P, 2, T]),
                                          ALU.subtract).then_inc(centred, 1)
                    for unit in units:
                        split(unit, unit % SLOTS)
                    if scale is not None:
                        finish_vector(scale)
                        dve.wait_ge(mod_read, l * NMOD + (scale + 2))
                        coefficients(shift, scale, ln_gT[:, i], ln_bT[:, i])
                    dve.wait_ge(centred, (l * 3 + (i + 1)) * (DT // 2))
                    dve.wait_ge(std_ready, l * 3 + (i + 1))
                    own.did(dve.reciprocal(rstd[:], rstd[:]))
                    own.wait()
                    for m in range(DT):
                        o = dve.tensor_tensor(z[:, m, 0:TP], z[:, m, 0:TP], rstd[:, 0:TP], ALU.mult)
                        if m == 0:
                            own.did(o)
                            dve.tensor_tensor(z[:, :, TP:T], z[:, :, TP:T],
                                              rstd[:, TP:T].unsqueeze(1).broadcast_to([P, DT, B]), ALU.mult)\
                               .then_inc(normed, 1)
                            if scale is not None:
                                dve.wait_ge(normed, l * (3 * DT) + ((i + 1) * DT + 1))
                                modulate_samples(i + 2)
                        else:
                            o.then_inc(normed, 1)

                def negative_lambda():
                    own.did(dve.tensor_scalar(sp[:, 2], lamT, -1.0, None, ALU.mult))
                    own.wait()
                    dve.tensor_tensor(sp[:, 3], sp[:, 2], lamT, ALU.min).then_inc(lam_ready, 1)
                    dve.wait_ge(lam_ready, l + 1)

                def softplus():
                    own.did(dve.tensor_scalar(sp[:, 2], sp[:, 2], 0.0, None, ALU.max))
                    dve.wait_ge(lam_exp, l + 1)
                    e, zz, z2, p = sp[:, 4], sp[:, 5], sp[:, 6], sp[:, 7]
                    own.then(dve.tensor_scalar(zz, e, 2.0, None, ALU.add))
                    own.then(dve.reciprocal(zz, zz))
                    own.then(dve.tensor_tensor(zz, zz, e, ALU.mult))
                    own.then(dve.tensor_tensor(z2, zz, zz, ALU.mult))
                    own.then(dve.tensor_scalar(p, z2, 1.0 / 17, None, ALU.mult))
                    for d in (15, 13, 11, 9, 7, 5, 3):
                        own.then(dve.scalar_tensor_tensor(p, p, 1.0 / d, z2, ALU.add, ALU.mult))
                    own.then(dve.scalar_tensor_tensor(p, p, 1.0, zz, ALU.add, ALU.mult))
                    own.then(dve.scalar_tensor_tensor(p, p, 2.0, sp[:, 2], ALU.mult, ALU.add))
                    own.did(dve.tensor_scalar(c8, p, LRU_C, None, ALU.mult))
                    own.did(dve.tensor_scalar(nc8, p, -LRU_C, None, ALU.mult))

                def feed_forward(f, gate, between):
                    with dve.Fori(0, UP_UNITS // SLOTS) as r:
                        for j in range(SLOTS):
                            n = UP[f] + j + 2
                            split(r * SLOTS + n, n % SLOTS)
                            turn = l * (2 * FT) + r * SLOTS + (f * FT + j + 1)
                            dve.wait_ge(units_done, l * UNITS + r * SLOTS + (UP[f] + j + 1 + SLOTS))
                            dve.wait_ge(gate_read, turn + 3)
                            dve.wait_ge(h_ready, turn)
                            dve.tensor_tensor(h_full[:], gate_act[:], bank[2 * j + 1][:, 0:T], ALU.mult)\
                               .then_inc(up_read, 1)
                            dve.wait_ge(h_hi_done, turn)
                            dve.tensor_tensor(h_lo[:, r * SLOTS + j], h_full[:],
                                              h_hi[:, r * SLOTS + j].bitcast(F32), ALU.subtract)\
                               .then_inc(h_ready, 1)
                    for i in range(DOWN_UNITS):
                        n = DOWN[f] + i + 2
                        if n < UNITS and i < DOWN_UNITS - 1:
                            split(n, n % SLOTS)
                        if i == 0 and f == 0:
                            negative_lambda()
                        if i == 1:
                            finish_vector(between[0])
                        if i == 3 and f == 0:
                            softplus()
                        if i == 5 and len(between) > 1:
                            finish_vector(between[1])
                        if i % 3 == 2:
                            pair = i // 3
                            dve.wait_ge(units_done, l * UNITS + (DOWN[f] + i + 1 + SLOTS))
                            residual([(2 * pair + i, 2 * (pair % 2) + i) for i in range(2)], gate,
                                     (pair_read, l * 8 + (f * 4 + pair + 1 + 2)), 0, DT - 1)

                split(0, 0)
                dve.wait_ge(prep_out, l + 1)
                own.did(dve.tensor_copy(pT[:], bank[1][:, 128:248]))
                own.wait()
                scales = bias_mod[:, SC1::SC2 - SC1]
                own.did(dve.tensor_scalar(scales, scales, 1.0, None, ALU.add))
                own.did(dve.tensor_copy(qT[:], bank[1][:, 248:284]))
                own.wait()
                finish_vector(S1)
                dve.wait_ge(half_out, l + 1)
                own.did(dve.tensor_tensor(mod[:, SC1, 0:4], half_turned(SC1, 0), bias(SC1, 0, 4), ALU.add))
                dve.wait_ge(mod_read, l * NMOD + (S1 + 2))
                coefficients(S1, SC1, last_ln[:, 0], last_ln[:, 1], 0, 4)
                modulate_samples(0, 0, 4)
                turned = bank[1][:, 0:WT * 32].rearrange("p (m r) -> p m r", r=32)
                for m in range(WT):
                    own.did(dve.tensor_copy(uls[:, m, :, 0:CW - 1],
                                            turned[:, m, 0:B * (CW - 1)].rearrange("p (b t) -> p b t", b=B)))
                dve.tensor_copy(h0[:], turned[:, :, 24:24 + B]).then_inc(prep_read, 1)
                for m in range(WT):
                    o = dve.tensor_copy(us[:, m, :, 0:BUF],
                                        bank[0][:, m * B * BUF:(m + 1) * B * BUF].rearrange("p (b t) -> p b t", b=B))
                    if m < WT - 1:
                        own.did(o)
                    else:
                        o.then_inc(prep_read, 1)
                dve.wait_ge(prep_read, (l + 1) * 2)
                split_input(0, 0, 4)
                finish_vector(SC1)
                dve.wait_ge(mod_read, l * NMOD + (SC1 + 2))
                coefficients(S1, SC1, last_ln[:, 0], last_ln[:, 1], 4, 4)
                modulate_samples(1, 4, 4)
                split_input(0, 4, 4)
                dve.wait_ge(x_ready, l * (3 * DT) + DT)
                own.did(dve.tensor_copy(last_ln[:, 0], ln_gT[:, 2]))
                own.did(dve.tensor_copy(last_ln[:, 1], ln_bT[:, 2]))
                split(1, 1)
                feed_forward(0, G1, [G1, S2])
                norm(0, S2, SC2, [IN + 1])
                split_input(1)

                own.did(dve.memset(up[:, :, 0:BUF], 0.0))
                own.did(dve.memset(ul[:, :, 0:CW - 1], 0.0))

                def convolve(tiles):
                    for m in tiles:
                        own.did(dve.tensor_scalar(xc[:, m, 0:TP], ul[:, m, 0:TP], cwT[:, 0, m:m + 1],
                                                  cbT[:, m:m + 1], ALU.mult, ALU.add))
                    own.wait()
                    for k in range(1, CW):
                        for m in tiles:
                            o = dve.scalar_tensor_tensor(xc[:, m, 0:TP], ul[:, m, k:k + TP], cwT[:, k, m:m + 1],
                                                         xc[:, m, 0:TP], ALU.mult, ALU.add)
                            if (k, m) == (CW - 1, WT - 1):
                                o.then_inc(xc_ready, 1)
                            else:
                                own.did(o)
                        own.wait()

                def convolve_samples():
                    taps = cwT.rearrange("p k m -> p m k").unsqueeze(2).broadcast_to([P, WT, B, CW])
                    own.then(dve.tensor_tensor(prod[:], uls[:], taps, ALU.mult))
                    own.then(dve.tensor_reduce(small[:], prod[:], AX_X, ALU.add))
                    dve.tensor_tensor(xc[:, :, TP:T], small[:], cbT.unsqueeze(2).broadcast_to([P, WT, B]), ALU.add)\
                       .then_inc(xc_ready, 1)

                def window_sums():
                    own.wait()
                    dve.wait_ge(up_copied, l * 2 + 2)

                    own.then(dve.tensor_tensor(win_a[:, :, 1:TP + BUF], up[:, :, 1:TP + BUF],
                                               up[:, :, 0:TP + BUF - 1], ALU.add))
                    for g, (dst, src) in ((1, (win_b, win_a)), (2, (win_a, win_b)), (3, (win_b, win_a))):
                        w = WINDOWS[g]
                        own.then(dve.tensor_tensor(dst[:, g:WT, w - 1:TP + BUF], src[:, g:WT, w - 1:TP + BUF],
                                                   src[:, g:WT, w // 2 - 1:TP + BUF - w // 2], ALU.add))

                def windows():
                    dve.wait_ge(x_ready, l * (3 * DT) + 2 * DT)
                    own.wait()
                    own.did(dve.tensor_copy(us[:, :, :, BUF], up[:, :, BUF + TP:]))
                    for g, w in enumerate(WINDOWS):
                        sums = (win_a, win_b)[g % 2][:, g, BUF:BUF + TP]
                        own.did(dve.scalar_tensor_tensor(z[:, g, 0:TP], sums, 1.0 / w, up[:, g, BUF:BUF + TP],
                                                         ALU.mult, ALU.subtract))
                    own.wait()
                    for g, w in enumerate(WINDOWS):
                        own.did(dve.tensor_tensor(z[:, g, 0:16], (win_a, win_b)[g % 2][:, g, BUF:BUF + 16],
                                                  inv_head[:, g], ALU.mult))
                        own.did(dve.tensor_reduce(small[:, g], us[:, g, :, BUF + 1 - w:BUF + 1], AX_X, ALU.add))
                    own.wait()
                    own.did(dve.tensor_tensor(z[:, 0:WT, 0:16], z[:, 0:WT, 0:16], up[:, :, BUF:BUF + 16],
                                              ALU.subtract))
                    for g, w in enumerate(WINDOWS):
                        o = dve.scalar_tensor_tensor(z[:, g, TP:T], small[:, g], 1.0 / w, us[:, g, :, BUF],
                                                     ALU.mult, ALU.subtract)
                        if g < WT - 1:
                            own.did(o)
                    o.then_inc(pooled_ready, 1)

                for i in range(4):
                    split(IN + i + 2, (IN + i + 2) % SLOTS)
                    if i < 2:
                        dve.wait_ge(units_done, l * UNITS + (IN + i + 1 + SLOTS))
                        own.did(dve.tensor_copy(up[:, 2 * i, BUF:BUF + T], bank[2 * i][:, 0:T]))
                        dve.tensor_copy(up[:, 2 * i + 1, BUF:BUF + T], bank[2 * i + 1][:, 0:T]).then_inc(up_copied, 1)
                own.wait()
                dve.wait_ge(ul_copied, l * 2 + 1)
                convolve((0, 1))
                dve.wait_ge(ul_copied, l * 2 + 2)
                own.then(dve.tensor_copy(uls[:, :, :, CW - 1], ul[:, :, CW - 1 + TP:]))
                convolve_samples()
                convolve((2, 3))
                finish_vector(G2)
                window_sums()
                windows()
                split(OUT, OUT % SLOTS)

                dve.wait_ge(sig_done, (l + 1) * (2 * WT))
                own.did(dve.tensor_tensor(ig[:], ig[:], xc[:], ALU.mult))
                dve.wait_ge(decay_done, (l + 1) * (2 * WT))
                own.then(dve.tensor_tensor(rg[:], av[:], av[:], ALU.mult))
                dve.scalar_tensor_tensor(tt[:], rg[:], 1.0, tt[:], ALU.add, ALU.mult).then_inc(ratio_ready, 1)
                own.did(dve.tensor_tensor(hs[:, :, TP:T], av[:, :, TP:T], h0[:], ALU.mult))
                dve.wait_ge(m_hi_done, l * (3 * DT + 2) + (2 * DT + 1))
                dve.tensor_tensor(m_lo[:, 0:WT], z[:, 0:WT], m_hi[:, 0:WT].bitcast(F32), ALU.subtract)\
                   .then_inc(m_ready, 1)
                split(OUT + 1, (OUT + 1) % SLOTS)
                dve.wait_ge(root_done, l + 1)
                own.then(dve.tensor_tensor(ig[:], ig[:], rg[:], ALU.mult))
                for m in range(WT):
                    own.did(dve.tensor_tensor_scan(hs[:, m, 0:TP], av[:, m, 0:TP], ig[:, m, 0:TP], 0.0,
                                                   ALU.mult, ALU.add))
                own.then(dve.tensor_tensor(hs[:, :, TP:T], hs[:, :, TP:T], ig[:, :, TP:T], ALU.add))
                own.wait()
                finish_vector(S3)
                split(OUT + 2, (OUT + 2) % SLOTS)
                dve.wait_ge(gelu_done, l + 1)
                dve.tensor_tensor(z[:, WT:], z[:, WT:], hs[:], ALU.mult).then_inc(ylru_done, 1)
                split(OUT + 3, (OUT + 3) % SLOTS)
                dve.wait_ge(m_hi_done, l * (3 * DT + 2) + (2 * DT + 2))
                dve.tensor_tensor(m_lo[:, WT:], z[:, WT:], m_hi[:, WT:].bitcast(F32), ALU.subtract)\
                   .then_inc(m_ready, 1)
                for i, (m0, n, kh) in enumerate(OUT_PLAN):
                    if 1 < i < OUT_UNITS - 2:
                        split(OUT + i + 2, (OUT + i + 2) % SLOTS)
                    if kh:
                        dve.wait_ge(units_done, l * UNITS + (OUT + i + 1 + SLOTS))
                        residual([(m, m) for m in range(m0, m0 + n)], G2, (out_read, l * 3 + (i - 2)), 5, 1)

                def turn_rows():
                    for i, (b, n) in enumerate(((2, BUF + B), (3, CW - 1 + B), (4, 1 + B))):
                        dve.wait_ge(rows_out, l * 3 + i + 1)
                        dve.tensor_copy(s_rows[32 * i:32 * i + n, :], bank[b][0:n, :]).then_inc(rows_ready, 1)

                norm(1, S3, SC3, [UP[1], UP[1] + 1])
                split_input(2)
                turn_rows()
                feed_forward(1, G3, [G3])
                norm(2)
                assert own.n == VECTOR_STEPS, own.n

            with dve.Fori(0, DEPTH) as l:
                layer(l)

            for m in range(DT):
                dve.wait_ge(fin_out, m + 1)
                dve.tensor_copy(ys_rows[:, m * P:(m + 1) * P], bank[m][0:B, TP:TP + P]).then_inc(fin_read, 1)
                dve.tensor_copy(x_rows[:, :, m * P:(m + 1) * P],
                                bank[m][:, 0:TP].rearrange("p (a d) -> p a d", a=2)).then_inc(fin_read, 1)


_INS = ['x_prompt', 'x_sample', 'state_pool', 'state_conv', 'state_rglru', 'c_prompt', 'c_sample', 'w_ada', 'b_ada',
        'ffn1_wgu', 'ffn1_wdown', 'w_in', 'w_out', 'w_pool', 'pool_scale', 'conv_w', 'conv_b', 'w_rg_a', 'b_rg_a',
        'w_rg_x', 'b_rg_x', 'lru_lambda', 'ffn2_wgu', 'ffn2_wdown', 'ln_g', 'ln_b']


def kernel(**inputs):
    import numpy as _np
    import concourse.bacc as _bacc
    from concourse import mybir as _mybir
    from concourse.bass_utils import run_bass_kernel_spmd as _run

    depth, decs, buf, width = inputs['state_pool'].shape
    cw1 = inputs['state_conv'].shape[2]
    outs = [tuple(inputs['x_prompt'].shape), tuple(inputs['x_sample'].shape), (depth, 1, buf, width),
            (depth, 1, cw1, width), (depth, 1, width), (depth, decs, buf, width), (depth, decs, cw1, width),
            (depth, decs, width)]
    nc = _bacc.Bacc("TRN2", target_bir_lowering=False, num_devices=1)
    arrays, args = {}, []
    for name in _INS:
        a = _np.ascontiguousarray(inputs[name])
        arrays[f"in_{name}_dram"] = a
        args.append(nc.dram_tensor(f"in_{name}_dram", a.shape, _mybir.dt.from_np(a.dtype), kind="ExternalInput").ap())
    for i, shape in enumerate(outs):
        args.append(nc.dram_tensor(f"out_{i}_dram", shape, _mybir.dt.float32, kind="ExternalOutput").ap())
    trunk(nc, *args)
    r = _run(nc, [arrays], core_ids=[0])
    return tuple(r.results[0][f"out_{i}_dram"] for i in range(len(outs)))
```
